# Optimizing a Trainium2 kernel written in Bass

```python
import jax
import jax.numpy as jnp
from jax import lax
import numpy as np

D_MODEL = 1024
BATCH = 1
SEQ = 256
DEPTH = 1
DEC_BATCH = 8
DEC_SEQ = 16
PAST_LEN = 256

CHUNK = 64
Q_BLOCK = 128
N_MEM = 256
H_MLA = 8
Q_LORA = 256
KV_LORA = 128
NOPE_DIM = 64
ROPE_DIM = 32
V_DIM = 64
ROPE_THETA = 10000.0
MLA_SCALE = (NOPE_DIM + ROPE_DIM) ** -0.5
H_FOX = 8
HD_FOX = 64
FOX_SCALE = HD_FOX ** -0.5
FORGET_BIAS_INIT = 3.0
H_MEM = 4
HD_MEM = 128
MEM_SCALE = HD_MEM ** -0.5
N_BRANCH = 3
N_EXPERTS = 64
TOP_K = 8
N_GROUPS = 8
TOPK_GROUPS = 4
D_EXPERT = 256
D_SHARED = 256
ROUTED_SCALE = 2.5
ALPHA = (2 * DEPTH) ** 0.25
BETA = (8 * DEPTH) ** -0.25
NORM_EPS = 1e-5
NEG_INF = -1e30
IN_WIDTHS = (Q_LORA, KV_LORA, ROPE_DIM, H_FOX * HD_FOX, H_FOX * HD_FOX, H_FOX * HD_FOX, H_FOX,
             H_MEM * HD_MEM, N_BRANCH * D_MODEL)
D_IN = sum(IN_WIDTHS)

kernel_name = "hybrid_mla_fox_memory_moe_stream_step"

def layer_norm(x, g, b):
    xf = x.astype(jnp.float32)
    mu = jnp.mean(xf, axis=-1, keepdims=True)
    var = jnp.mean(jnp.square(xf - mu), axis=-1, keepdims=True)
    y = (xf - mu) * lax.rsqrt(var + NORM_EPS) * g.astype(jnp.float32) + b.astype(jnp.float32)
    return y.astype(x.dtype)

def rms_norm(x, g):
    xf = x.astype(jnp.float32)
    ms = jnp.mean(jnp.square(xf), axis=-1, keepdims=True)
    return (xf * lax.rsqrt(ms + NORM_EPS) * g.astype(jnp.float32)).astype(x.dtype)

def rope(x, pos):
    half = x.shape[-1] // 2
    inv_freq = ROPE_THETA ** (-jnp.arange(half, dtype=jnp.float32) / half)
    ang = pos.astype(jnp.float32)[:, None] * inv_freq[None, :]
    shape = (pos.shape[0],) + (1,) * (x.ndim - 3) + (half,)
    cos = jnp.cos(ang).reshape(shape).astype(x.dtype)
    sin = jnp.sin(ang).reshape(shape).astype(x.dtype)
    x1, x2 = x[..., :half], x[..., half:]
    return jnp.concatenate([x1 * cos - x2 * sin, x1 * sin + x2 * cos], axis=-1)

def project_in(h, pos, w_in, b_f, q_norm_g, w_q_up, kv_norm_g, w_kv_up):
    b, s, _ = h.shape
    split_points = np.cumsum(IN_WIDTHS)[:-1].tolist()
    q_lat, c_kv, k_r, f_q, f_k, f_v, f_logit, m_q, g = jnp.split(h @ w_in, split_points, axis=-1)
    q = (rms_norm(q_lat, q_norm_g) @ w_q_up).reshape(b, s, H_MLA, NOPE_DIM + ROPE_DIM)
    q_nope = q[..., :NOPE_DIM]
    q_rope = rope(q[..., NOPE_DIM:], pos)
    latent = rms_norm(c_kv, kv_norm_g)
    k_rope = rope(k_r, pos)
    f_q = f_q.reshape(b, s, H_FOX, HD_FOX)
    f_k = f_k.reshape(b, s, H_FOX, HD_FOX)
    f_v = f_v.reshape(b, s, H_FOX, HD_FOX)
    log_f = jax.nn.log_sigmoid((f_logit + b_f).astype(jnp.float32))
    m_q = m_q.reshape(b, s, H_MEM, HD_MEM)
    gates = jax.nn.sigmoid(g.astype(jnp.float32)).astype(h.dtype).reshape(b, s, N_BRANCH, D_MODEL)
    return q_nope, q_rope, latent, k_rope, f_q, f_k, f_v, log_f, m_q, gates

def mla_expand(latent, w_kv_up):
    b, l, _ = latent.shape
    kv = (latent @ w_kv_up).reshape(b, l, H_MLA, NOPE_DIM + V_DIM)
    return kv[..., :NOPE_DIM], kv[..., NOPE_DIM:]

def masked_softmax(s, mask):
    return jax.nn.softmax(jnp.where(mask, s.astype(jnp.float32), NEG_INF), axis=-1)

def attend_block(q_nope, q_rope, f_q, c_q, m_q, q_pos,
                 k_nope, k_rope, v_mla, f_k, f_v, c_k, k_pos, m_k, m_v):
    s = (jnp.einsum('bqhd,bkhd->bhqk', q_nope, k_nope)
         + jnp.einsum('bqhr,bkr->bhqk', q_rope, k_rope)) * MLA_SCALE
    chunk_mask = (k_pos[None, :] // CHUNK) <= (q_pos[:, None] // CHUNK)
    p = masked_softmax(s, chunk_mask).astype(v_mla.dtype)
    o_mla = jnp.einsum('bhqk,bkhd->bqhd', p, v_mla)
    s = jnp.einsum('bqhd,bkhd->bhqk', f_q, f_k).astype(jnp.float32) * FOX_SCALE
    s = s + (jnp.swapaxes(c_q, 1, 2)[..., :, None] - jnp.swapaxes(c_k, 1, 2)[..., None, :])
    causal = k_pos[None, :] <= q_pos[:, None]
    p = masked_softmax(s, causal).astype(f_v.dtype)
    o_fox = jnp.einsum('bhqk,bkhd->bqhd', p, f_v)
    s = jnp.einsum('bqhd,bmhd->bhqm', m_q, m_k).astype(jnp.float32) * MEM_SCALE
    p = jax.nn.softmax(s, axis=-1).astype(m_v.dtype)
    o_mem = jnp.einsum('bhqm,bmhd->bqhd', p, m_v)
    return o_mla, o_fox, o_mem

def merge_branches(o_mla, o_fox, o_mem, gates, w_br_mla, w_br_fox, w_br_mem, w_out):
    b, s = gates.shape[:2]
    y = (gates[:, :, 0] * (o_mla.reshape(b, s, -1) @ w_br_mla)
         + gates[:, :, 1] * (o_fox.reshape(b, s, -1) @ w_br_fox)
         + gates[:, :, 2] * (o_mem.reshape(b, s, -1) @ w_br_mem))
    return y @ w_out

def moe_ffn(x, w_router, router_bias, w_e_gate, w_e_up, w_e_down, w_s_gate, w_s_up, w_s_down):
    b, s, d = x.shape
    t = x.reshape(-1, d)
    scores = jax.nn.sigmoid((t @ w_router).astype(jnp.float32))
    sel = scores + router_bias.astype(jnp.float32)
    grp = sel.reshape(-1, N_GROUPS, N_EXPERTS // N_GROUPS)
    group_score = lax.top_k(grp, 2)[0].sum(-1)
    _, g_idx = lax.top_k(group_score, TOPK_GROUPS)
    g_mask = jax.nn.one_hot(g_idx, N_GROUPS, dtype=jnp.float32).sum(1) > 0
    e_mask = jnp.repeat(g_mask, N_EXPERTS // N_GROUPS, axis=1)
    _, e_idx = lax.top_k(jnp.where(e_mask, sel, -jnp.inf), TOP_K)
    w = jnp.take_along_axis(scores, e_idx, axis=1)
    w = w / jnp.sum(w, axis=-1, keepdims=True) * ROUTED_SCALE
    gate = jnp.sum(jax.nn.one_hot(e_idx, N_EXPERTS, dtype=jnp.float32) * w[..., None], axis=1)
    gate = gate.astype(x.dtype)

    def expert_step(acc, ew):
        wg, wu, wd, g_col = ew
        hid = jax.nn.silu(t @ wg) * (t @ wu)
        return acc + g_col[:, None] * (hid @ wd), None

    routed, _ = lax.scan(expert_step, jnp.zeros_like(t), (w_e_gate, w_e_up, w_e_down, gate.T))
    shared = (jax.nn.silu(t @ w_s_gate) * (t @ w_s_up)) @ w_s_down
    return (routed + shared).reshape(b, s, d)

def post_norm_block(h, mixer_out, ln1_g, ln1_b, ln2_g, ln2_b, moe_w):
    x1 = layer_norm(ALPHA * h + mixer_out, ln1_g, ln1_b)
    return layer_norm(ALPHA * x1 + moe_ffn(x1, *moe_w), ln2_g, ln2_b)

def to_blocks(a):
    b, s = a.shape[:2]
    return jnp.swapaxes(a.reshape(b, s // Q_BLOCK, Q_BLOCK, *a.shape[2:]), 0, 1)

def from_blocks(a):
    nb, b, qb = a.shape[:3]
    return jnp.swapaxes(a, 0, 1).reshape(b, nb * qb, *a.shape[3:])

def setup_inputs(seed: int = 0) -> dict:
    key = jax.random.key(seed)
    ks = jax.random.split(key, 40)
    f32 = jnp.float32

    def nrm(k, shape, scale=1.0):
        return jax.random.normal(k, shape, f32) * scale

    L = DEPTH
    return {
        "x_prompt": nrm(ks[0], (BATCH, SEQ, D_MODEL)),
        "x_sample": nrm(ks[1], (DEC_BATCH, DEC_SEQ, D_MODEL)),
        "mem_prompt": nrm(ks[2], (BATCH, N_MEM, D_MODEL)),
        "cache_mla_latent": nrm(ks[3], (L, DEC_BATCH, PAST_LEN, KV_LORA)),
        "cache_mla_krope": nrm(ks[4], (L, DEC_BATCH, PAST_LEN, ROPE_DIM)),
        "cache_fox_k": nrm(ks[5], (L, DEC_BATCH, PAST_LEN, H_FOX, HD_FOX)),
        "cache_fox_v": nrm(ks[6], (L, DEC_BATCH, PAST_LEN, H_FOX, HD_FOX)),
        "cache_fox_logf": jax.nn.log_sigmoid(FORGET_BIAS_INIT + nrm(ks[7], (L, DEC_BATCH, PAST_LEN, H_FOX))),
        "cache_mem_k": nrm(ks[8], (L, DEC_BATCH, N_MEM, H_MEM, HD_MEM)),
        "cache_mem_v": nrm(ks[9], (L, DEC_BATCH, N_MEM, H_MEM, HD_MEM)),
        "ln1_g": 1.0 + nrm(ks[10], (L, D_MODEL), 0.01),
        "ln1_b": nrm(ks[11], (L, D_MODEL), 0.01),
        "w_in": nrm(ks[12], (L, D_MODEL, D_IN), D_MODEL ** -0.5),
        "b_f": FORGET_BIAS_INIT + nrm(ks[13], (L, H_FOX), 0.1),
        "q_norm_g": 1.0 + nrm(ks[14], (L, Q_LORA), 0.01),
        "w_q_up": nrm(ks[15], (L, Q_LORA, H_MLA * (NOPE_DIM + ROPE_DIM)), Q_LORA ** -0.5),
        "kv_norm_g": 1.0 + nrm(ks[16], (L, KV_LORA), 0.01),
        "w_kv_up": nrm(ks[17], (L, KV_LORA, H_MLA * (NOPE_DIM + V_DIM)), KV_LORA ** -0.5),
        "w_mem_k": nrm(ks[18], (L, D_MODEL, H_MEM * HD_MEM), D_MODEL ** -0.5),
        "w_mem_v": nrm(ks[19], (L, D_MODEL, H_MEM * HD_MEM), D_MODEL ** -0.5),
        "w_br_mla": nrm(ks[20], (L, H_MLA * V_DIM, D_MODEL), BETA * (H_MLA * V_DIM) ** -0.5),
        "w_br_fox": nrm(ks[21], (L, H_FOX * HD_FOX, D_MODEL), BETA * (H_FOX * HD_FOX) ** -0.5),
        "w_br_mem": nrm(ks[22], (L, H_MEM * HD_MEM, D_MODEL), BETA * (H_MEM * HD_MEM) ** -0.5),
        "w_out": nrm(ks[23], (L, D_MODEL, D_MODEL), BETA * D_MODEL ** -0.5),
        "ln2_g": 1.0 + nrm(ks[24], (L, D_MODEL), 0.01),
        "ln2_b": nrm(ks[25], (L, D_MODEL), 0.01),
        "w_router": nrm(ks[26], (L, D_MODEL, N_EXPERTS), D_MODEL ** -0.5),
        "router_bias": nrm(ks[27], (L, N_EXPERTS), 0.01),
        "w_e_gate": nrm(ks[28], (L, N_EXPERTS, D_MODEL, D_EXPERT), D_MODEL ** -0.5),
        "w_e_up": nrm(ks[29], (L, N_EXPERTS, D_MODEL, D_EXPERT), D_MODEL ** -0.5),
        "w_e_down": nrm(ks[30], (L, N_EXPERTS, D_EXPERT, D_MODEL), BETA * D_EXPERT ** -0.5),
        "w_s_gate": nrm(ks[31], (L, D_MODEL, D_SHARED), D_MODEL ** -0.5),
        "w_s_up": nrm(ks[32], (L, D_MODEL, D_SHARED), D_MODEL ** -0.5),
        "w_s_down": nrm(ks[33], (L, D_SHARED, D_MODEL), BETA * D_SHARED ** -0.5),
    }

def reference(x_prompt, x_sample, mem_prompt, cache_mla_latent, cache_mla_krope, cache_fox_k,
              cache_fox_v, cache_fox_logf, cache_mem_k, cache_mem_v, ln1_g, ln1_b, w_in, b_f,
              q_norm_g, w_q_up, kv_norm_g, w_kv_up, w_mem_k, w_mem_v, w_br_mla, w_br_fox,
              w_br_mem, w_out, ln2_g, ln2_b, w_router, router_bias, w_e_gate, w_e_up, w_e_down,
              w_s_gate, w_s_up, w_s_down):
    pos_p = jnp.arange(SEQ, dtype=jnp.int32)
    q_pos_s = PAST_LEN + jnp.arange(DEC_SEQ, dtype=jnp.int32)
    k_pos_s = jnp.arange(PAST_LEN + DEC_SEQ, dtype=jnp.int32)
    h_p, h_s = x_prompt, x_sample
    p_lat, p_kr, p_fk, p_fv, p_lf, p_mk, p_mv = [], [], [], [], [], [], []
    s_lat, s_kr, s_fk, s_fv, s_lf = [], [], [], [], []

    for l in range(DEPTH):
        mix_w = (w_in[l], b_f[l], q_norm_g[l], w_q_up[l], kv_norm_g[l], w_kv_up[l])
        merge_w = (w_br_mla[l], w_br_fox[l], w_br_mem[l], w_out[l])
        moe_w = (w_router[l], router_bias[l], w_e_gate[l], w_e_up[l], w_e_down[l],
                 w_s_gate[l], w_s_up[l], w_s_down[l])
        norm_w = (ln1_g[l], ln1_b[l], ln2_g[l], ln2_b[l])

        q_nope, q_rope, lat, k_rope, f_q, f_k, f_v, log_f, m_q, gates = project_in(h_p, pos_p, *mix_w)
        k_nope, v_mla = mla_expand(lat, w_kv_up[l])
        c_f = jnp.cumsum(log_f, axis=1)
        m_k = (mem_prompt @ w_mem_k[l]).reshape(BATCH, N_MEM, H_MEM, HD_MEM)
        m_v = (mem_prompt @ w_mem_v[l]).reshape(BATCH, N_MEM, H_MEM, HD_MEM)
        outs = lax.map(
            lambda qb: attend_block(*qb, k_nope, k_rope, v_mla, f_k, f_v, c_f, pos_p, m_k, m_v),
            (to_blocks(q_nope), to_blocks(q_rope), to_blocks(f_q), to_blocks(c_f), to_blocks(m_q),
             pos_p.reshape(-1, Q_BLOCK)))
        o_mla, o_fox, o_mem = (from_blocks(o) for o in outs)
        mix = merge_branches(o_mla, o_fox, o_mem, gates, *merge_w)
        p_lat.append(lat)
        p_kr.append(k_rope)
        p_fk.append(f_k)
        p_fv.append(f_v)
        p_lf.append(log_f.astype(h_p.dtype))
        p_mk.append(m_k)
        p_mv.append(m_v)
        h_p = post_norm_block(h_p, mix, *norm_w, moe_w)

        q_nope, q_rope, lat, k_rope, f_q, f_k, f_v, log_f, m_q, gates = project_in(h_s, q_pos_s, *mix_w)
        lat_all = jnp.concatenate([cache_mla_latent[l], lat], axis=1)
        kr_all = jnp.concatenate([cache_mla_krope[l], k_rope], axis=1)
        k_nope, v_mla = mla_expand(lat_all, w_kv_up[l])
        fk_all = jnp.concatenate([cache_fox_k[l], f_k], axis=1)
        fv_all = jnp.concatenate([cache_fox_v[l], f_v], axis=1)
        c_all = jnp.cumsum(jnp.concatenate([cache_fox_logf[l].astype(jnp.float32), log_f], axis=1), axis=1)
        o_mla, o_fox, o_mem = attend_block(q_nope, q_rope, f_q, c_all[:, PAST_LEN:], m_q, q_pos_s,
                                           k_nope, kr_all, v_mla, fk_all, fv_all, c_all, k_pos_s,
                                           cache_mem_k[l], cache_mem_v[l])
        mix = merge_branches(o_mla, o_fox, o_mem, gates, *merge_w)
        s_lat.append(lat)
        s_kr.append(k_rope)
        s_fk.append(f_k)
        s_fv.append(f_v)
        s_lf.append(log_f.astype(h_s.dtype))
        h_s = post_norm_block(h_s, mix, *norm_w, moe_w)

    return (h_p, h_s,
            jnp.stack(p_lat), jnp.stack(p_kr), jnp.stack(p_fk), jnp.stack(p_fv), jnp.stack(p_lf),
            jnp.stack(p_mk), jnp.stack(p_mv),
            jnp.stack(s_lat), jnp.stack(s_kr), jnp.stack(s_fk), jnp.stack(s_fv), jnp.stack(s_lf))


_drawn_inputs = setup_inputs


def setup_inputs(seed=0):
    import zlib

    import numpy as np

    out = dict(_drawn_inputs(seed))
    spreads = {}
    factors = {'q_norm_g': 8.0,
     'kv_norm_g': 5.475,
     'ln2_g': 32.478,
     'ln2_b': 31.974,
     'cache_fox_logf': 3.399}
    for name, (base, spread) in spreads.items():
        noise = np.random.default_rng([zlib.crc32(name.encode()), seed]).standard_normal(out[name].shape)
        drawn = base * np.exp(spread * noise) if base else spread * noise
        out[name] = jnp.asarray(drawn.astype(out[name].dtype))
    for name, factor in factors.items():
        out[name] = (out[name] * factor).astype(out[name].dtype)
    return out
```

```python
from contextlib import ExitStack

import numpy as np

import concourse.bass as bass
from concourse import mybir

F32 = mybir.dt.float32
I32 = mybir.dt.int32
ALU = mybir.AluOpType
ACT = mybir.ActivationFunctionType
AX = mybir.AxisListType.X

P = 128
D = 1024
KD = D // P
SEQ, NB, NQ, PAST, NMEM = 256, 8, 16, 256, 256
TT = 3
T = TT * P
H, HM = 8, 4
QL, KVL, RD, ND = 256, 128, 32, 64
CHUNK = 64
E, TOPK, NG, TG = 64, 8, 8, 4
FE = 256
CAP = 96
ROUNDS = T // CAP
ALPHA = 2.0 ** 0.25
EPS = 1e-5
NEG = -1e30
MLA_SCALE = float(96 ** -0.5)
FOX_SCALE = 0.125
MEM_SCALE = float(128 ** -0.5)
OFF = {}
_o = 0
for _n, _w in (("qlat", 256), ("ckv", 128), ("kr", 32), ("fq", 512), ("fk", 512), ("fv", 512), ("fl", 8), ("mq", 512), ("g", 3072)):
    OFF[_n] = _o
    _o += _w

CST = {}
_c = 0
for _n, _w in (("ident", 128), ("tri", 128), ("ones", 256), ("blk", 128), ("strict", 128), ("causal", 128),
               ("chunk", 128), ("wfox", 240), ("wmla", 240), ("rope", 96), ("iota", CAP), ("tok", 3),
               ("oh", 8), ("eps", 1), ("slot0", 64), ("before", 64)):
    CST[_n] = (_c, _w)
    _c += _w
NCST = _c


def constants():
    c = np.zeros((P, NCST), np.float32)

    def put(name, a):
        o, w = CST[name]
        c[:a.shape[0], o:o + w] = a
    s = np.arange(P)[:, None]
    t = np.arange(P)[None, :]
    put("ident", np.eye(P))
    put("tri", s <= t)
    put("ones", np.ones((P, 256)))
    put("blk", (s // NQ == t // NQ) & (s <= t))
    put("strict", s < t)
    put("causal", np.where(t <= s, 0.0, NEG))
    put("chunk", np.where(t // CHUNK <= s // CHUNK, 0.0, NEG))
    w = np.arange(240)[None, :] - 7 * NQ
    own = (w >= 0) & (w < NQ)
    put("wfox", np.where(own & (w <= s % NQ), 0.0, NEG))
    put("wmla", np.where(own & (s >= 0), 0.0, NEG))
    half = RD // 2
    inv = np.float32(10000.0) ** (-np.arange(half, dtype=np.float32) / np.float32(half))
    pos = np.concatenate([np.arange(SEQ), PAST + np.arange(P) % NQ]).astype(np.float32)
    ang = (pos[:, None] * inv[None, :]).astype(np.float32)
    cs = np.concatenate([np.cos(ang), np.sin(ang)], 1).reshape(TT, P, RD).transpose(1, 0, 2)
    put("rope", cs.reshape(P, TT * RD))
    put("iota", np.broadcast_to(np.arange(CAP), (P, CAP)))
    put("tok", s + P * np.arange(TT)[None, :])
    oh = np.zeros((40, 8))
    oh[0:8] = np.eye(8)
    oh[32:40] = np.eye(8)
    put("oh", oh)
    put("eps", np.full((P, 1), EPS))
    put("slot0", np.broadcast_to(np.arange(E) * CAP, (P, E)))
    put("before", np.broadcast_to((np.arange(8)[None, :] < np.arange(8)[:, None]).reshape(1, 64), (P, 64)))
    return c


def units():
    u = []
    for h in range(H):
        for q in range(2):
            u.append(("mla", "p", h, q, P, (q + 1) * P))
    for h in range(H):
        for q in range(2):
            u.append(("fox", "p", h, q, P, (q + 1) * P))
    for h in range(HM):
        for q in range(2):
            u.append(("mem", "p", h, q, P, NMEM))
    for b in range(NB):
        u += [("mla", "s", b, 0, P, 3 * P), ("fox", "s", b, 0, P, 3 * P), ("mem", "s", b, 0, 64, NMEM)]
    return u


def w_units():
    w = []

    def both(name, col, n):
        w.append((name, 0, col, n))
        w.append((name, 4, col, n))
    both("lat", 0, 416)
    both("in", OFF["fk"], 512)
    both("in", OFF["fv"], 512)
    both("in", OFF["fq"], 512)
    both("in", OFF["mq"], 512)
    both("mem_k", 0, 512)
    both("mem_v", 0, 512)
    for br in range(3):
        for cb in range(2):
            both("in", OFF["g"] + br * D + cb * 512, 512)
            w.append((("br_mla", "br_fox", "br_mem")[br], 0, cb * 512, 512))
    both("out", 0, 512)
    both("out", 512, 512)
    w += [("s_gate",), ("s_up",), ("s_down",)]
    return w


def plan():
    U = units()
    s = []
    for j in range(TT):
        for half in range(2):
            s.append(("T", "x", j, half))
    for j in range(TT):
        s.append(("P", "lat", j))
    s.append(("rms",))
    for j in range(2):
        for half in range(2):
            s.append(("T", "mem", j, half))
    s += [("T", "uk", 0), ("T", "uk", 1)]
    s += [("P", "fk", j) for j in range(TT)]
    s += [("P", "fv", j) for j in range(TT)]
    s += [("T", "lat", j) for j in range(TT)]
    for j in range(TT):
        s.append(("P", "qr", j))
        s.append(("qrope", j))
        s.append(("T", "fk", j))
        s.append(("T", "qr", j, 0))
        s.append(("T", "qr", j, 1))
    s += [("P", "fq", m) for m in range(4)]
    for h in range(H):
        s.append(("P", "qn", h))
        if h:
            s.append(("P", "qa", h - 1))
    s.append(("P", "qa", H - 1))
    s += [("P", "mq", m) for m in range(4)]
    s += [("P", "mk", j) for j in range(2)]
    s += [("P", "mv", j) for j in range(2)]
    s += [("T", "mk", j) for j in range(2)]
    s.append(("V", "c", "p"))

    def load_keys(n):
        k, g, b = U[n][:3]
        if g != "s":
            return
        if k == "mla":
            s.append(("T", "clat", b))
        elif k == "fox":
            s.append(("T", "cfk", b, 0))
            s.append(("T", "cfk", b, 1))
            s.append(("V", "c", b))
        else:
            s.append(("T", "cmk", b, 0))
            s.append(("T", "cmk", b, 1))
    n_u = len(U)
    for n in range(n_u + 4):
        if n < n_u:
            load_keys(n)
            s.append(("prep", n))
            s.append(("S", n))
        if 1 <= n <= n_u:
            s.append(("norm", n - 1))
        if 2 <= n <= n_u + 1:
            s.append(("T", "p", n - 2))
        if 3 <= n <= n_u + 2:
            s.append(("V", "o", n - 3))
        if n >= 4 and U[n - 4][0] == "mla":
            s.append(("V", "ov", n - 4))
    for br in range(3):
        for cb in range(2):
            for j in range(TT):
                s.append(("P", "g", br, cb, j))
                s.append(("V", "b", br, cb, j))
    for j in range(TT):
        for half in range(2):
            s.append(("T", "y", j, half))
    for half in range(2):
        for j in range(TT):
            s.append(("V", "out", j, half))
    s.append(("ln1",))
    for j in range(TT):
        for half in range(2):
            s.append(("T", "x1", j, half))
    for j in range(TT):
        s.append(("V", "router", j))
    for m in range(4):
        s.append(("P", "sh", m))
    s.append(("route",))
    for j in range(TT):
        s.append(("V", "pos", j))
    s.append(("tables",))
    s.append(("V", "flag"))
    s.append(("shact",))
    for j in range(TT):
        for half in range(2):
            s.append(("V", "shd", j, half))
    return s


def build(nc, a, outs):
    U = units()
    PLAN = plan()
    WU = w_units()
    NW = 4
    pos_in = {}
    count = {"P": 0, "S": 0, "T": 0, "V": 0}
    for st in PLAN:
        if st[0] in count:
            pos_in[st] = count[st[0]]
            count[st[0]] += 1

    def done_at(*st):
        return pos_in[st] + 1

    last_use = []
    names = ["lat", "fk", "fv", "fq", "mq", "mk", "mv"]
    for nme in names:
        lu = {"lat": ("P", "lat", 2), "fk": ("P", "fk", 2), "fv": ("P", "fv", 2), "fq": ("P", "fq", 3),
              "mq": ("P", "mq", 3), "mk": ("P", "mk", 1), "mv": ("P", "mv", 1)}[nme]
        last_use += [lu, lu]
    for br in range(3):
        for cb in range(2):
            last_use += [("P", "g", br, cb, 2), ("P", "g", br, cb, 2), ("V", "b", br, cb, 2)]
    last_use += [("V", "out", 2, 0), ("V", "out", 2, 0), ("V", "out", 2, 1), ("V", "out", 2, 1)]
    last_use += [("P", "sh", 1), ("P", "sh", 3), ("V", "shd", 2, 1)]
    assert len(last_use) == len(WU)
    E_STORES = 12
    first_of = {"lat": 0, "fk": 2, "fv": 4, "fq": 6, "mq": 8, "mk": 10, "mv": 12, "g": 14, "out": 32, "s_gate": 36, "s_up": 37, "s_down": 38}

    with ExitStack() as ctx:
        def region(name, cols):
            return ctx.enter_context(nc.sbuf_tensor(name, [P, cols], F32))

        def sem(name):
            return ctx.enter_context(nc.semaphore(name))

        class Space:

            def __init__(self, reg, cols, at=0):
                self.reg, self.cols, self.at = reg, cols, at

            def take(self, *shape):
                n = int(np.prod(shape))
                v = self.reg[:, self.at:self.at + n]
                self.at += n
                assert self.at <= self.cols, (self.at, self.cols)
                if len(shape) == 2:
                    v = v.rearrange("p (a b) -> p a b", b=shape[1])
                if len(shape) == 3:
                    v = v.rearrange("p (a b c) -> p a b c", b=shape[1], c=shape[2])
                return v

        cst = region("cst", NCST)
        lngb_cols, o_cols, y_cols, w_cols, a_cols, m_cols = 2048, 4608, 3072, NW * 2048, 24576, 2660
        lngb = region("lngb", lngb_cols)
        x_sb = region("x_sb", 3072)[:, :].rearrange("p (j d) -> p j d", j=TT)
        xT = region("xT", 3072)[:, :].rearrange("p (k t) -> p k t", k=KD)
        R_O = region("branch_out", o_cols)
        R_Y = region("merge", y_cols)
        R_W = region("weight_ring", w_cols)
        R_A = region("arena", a_cols)
        R_M = region("small", m_cols)
        idx = ctx.enter_context(nc.sbuf_tensor("idx", [P, 4], I32))
        row_idx = ctx.enter_context(nc.sbuf_tensor("row_idx", [P, TT * TOPK], I32))
        flag_i = ctx.enter_context(nc.sbuf_tensor("flag_i", [1, 1], I32))

        def cc(name, rows=P):
            o, w = CST[name]
            return cst[0:rows, o:o + w]
        ident = cc("ident")
        rope_t = cc("rope").rearrange("p (j c) -> p j c", j=TT)

        wring = R_W[:, :].rearrange("p (s k n) -> p s k n", s=NW, k=4)
        oT = R_O[:, :].rearrange("p (r k t) -> p r k t", r=3, k=4)

        A = Space(R_A, a_cols)
        fqT = A.take(4, T)
        mqT = A.take(4, T)
        fkT = A.take(4, T)
        fv_tok = A.take(TT, 512)
        qabsP = A.take(H, 256)
        qabsS = A.take(NB, P)
        qrP = A.take(H, 256)
        qrS = A.take(NB, P)
        mv_tok = A.take(2, 512)
        mkT = A.take(HM, 256)
        w_kv = A.take(1024)
        late = A.at
        w_q = A.take(2, 768)
        lat_raw = A.take(TT, 424)
        fk_tok = A.take(TT, 512)
        qn = A.take(TT, 256)
        qnT = A.take(2, T)
        mk_tok = A.take(2, 512)
        wukT = A.take(H, P)
        OE = Space(R_O, o_cols)
        mem_sb = OE.take(2, D)
        memT = OE.take(KD, 256)
        YE = Space(R_Y, y_cols)
        qn_up = YE.take(2, T)
        qr_tok = YE.take(TT, 256)
        qr_rot = YE.take(TT, 256)
        scr = YE.take(256)
        gq_b = YE.take(256)
        gkv_b = YE.take(128)
        B = Space(R_A, a_cols, late)
        fkc = B.take(2, 512)
        mkc = B.take(2, 512)
        fvc = [B.take(2, 512) for _ in range(2)]
        mvc = [B.take(2, 512) for _ in range(2)]
        fkTc = B.take(4, 256)
        mkTc = B.take(4, 256)
        L = Space(lngb, lngb_cols)
        latc = [L.take(2, KVL) for _ in range(2)]
        krc = [L.take(2, RD) for _ in range(2)]
        latTc = L.take(256)
        krTc = L.take(256)
        latn = L.take(TT, KVL)
        latT = L.take(T)
        Y = Space(R_Y, y_cols)
        prob = [Y.take(T) for _ in range(3)]
        pT = [Y.take(T) for _ in range(2)]
        qbd_fox = Y.take(640)
        olat = [Y.take(P) for _ in range(2)]
        M = Space(R_M, m_cols)
        krT = M.take(T)
        kr_rot = M.take(TT, RD)
        mark_m = M.at
        lf_new = M.take(TT, 8)
        LFn = M.take(TT, 40)
        b_f_b = M.take(8)
        ssq = M.take(6)
        rst = M.take(6)
        lft = M.take(4, 24)
        rt = M.take(3, 128)
        mark_fr = M.at
        FR = M.take(T)
        FX = M.take(256)
        LH = M.take(256)
        qbd_mem = M.take(320)
        mx = M.take(len(U))
        sm = M.take(len(U))
        rs = M.take(len(U))
        C2 = Space(R_A, a_cols, B.at)
        lfc_raw = C2.take(16, 8)
        LFc = [C2.take(2, 40) for _ in range(2)]
        G = Space(R_M, m_cols, mark_fr)
        egate = [G.take(512) for _ in range(2)]
        y = R_Y[:, :].rearrange("p (j d) -> p j d", j=TT)
        yT = R_O[:, 0:3072].rearrange("p (k t) -> p k t", k=KD)

        N = Space(R_Y, y_cols)
        w_rt = N.take(KD, E)
        rb_b = N.take(E)
        sc, sel, masked, rep, mask, tmp3, slot_row = (N.take(TT, E) for _ in range(7))
        g8 = N.take(24, 8)
        gs, gm = N.take(24), N.take(24)
        TGP = N.take(TT, (E + 3) * 3)
        tgp4 = TGP.rearrange("p j (e c) -> p j e c", c=3)
        t8 = N.take(TT, TOPK)
        wsum = N.take(TT)
        cmax = N.take(1)
        pcol = [N.take(TT, 3) for _ in range(2)]
        gslot = N.take(4)
        XO = Space(R_O, o_cols)
        xgT = [XO.take(KD, CAP) for _ in range(2)]
        sil = [XO.take(2, CAP) for _ in range(2)]
        hid = [XO.take(2, CAP) for _ in range(2)]
        onehot = [XO.take(TT, CAP) for _ in range(2)]
        xg = [XO.take(D), Space(R_M, m_cols, mark_fr).take(D)]
        yo = [R_W[:, 3 * 2048 + i * D:3 * 2048 + (i + 1) * D] for i in range(2)]
        SH = Space(R_O, o_cols)
        sh_sil, sh_up = SH.take(2, T), SH.take(2, T)
        ew = [R_A[:, i * 6144:(i + 1) * 6144] for i in range(4)]
        ew_gate = [v[:, 0:2048].rearrange("p (k f) -> p k f", k=KD) for v in ew]
        ew_up = [v[:, 2048:4096].rearrange("p (k f) -> p k f", k=KD) for v in ew]
        ew_down = [v[:, 4096:6144].rearrange("p (m n) -> p m n", m=2) for v in ew]
        gathered_rows = R_A[:, :].rearrange("p (n d) -> p n d", d=D)
        sh_gate, sh_upw = (R_W[:, i * 2048:(i + 1) * 2048].rearrange("p (k f) -> p k f", k=KD) for i in range(2))
        sh_down = R_W[:, 4096:6144].rearrange("p (m n) -> p m n", m=2)
        x1_dram = nc.dram_tensor("x1_rows", (T, D), F32, kind="Internal").ap()
        y_dram = nc.dram_tensor("expert_rows", (E * CAP + 1, D), F32, kind="Internal").ap()

        ps = {r: [ctx.enter_context(nc.psum_tensor(f"ps_{r}{i}", [P, 512], F32)) for i in range(2)] for r in "PSTV"}
        done = {r: sem(f"{r}_done") for r in "PSTV"}
        free = {r: sem(f"{r}_free") for r in "PSTV"}

        w_loaded = [sem(f"w_loaded{i}") for i in range(NW)]
        x_loaded = [sem(f"x_loaded{j}") for j in range(TT)]
        cst_loaded = sem("cst_loaded")
        mem_loaded = [sem(f"mem_loaded{j}") for j in range(2)]
        up_loaded = sem("up_loaded")
        vec_loaded = sem("vec_loaded")
        logf_loaded = sem("logf_loaded")
        kcache = {k: sem(f"{k}_cache") for k in ("fk", "mk")}
        vcache = {k: [sem(f"{k}_cache{i}") for i in range(2)] for k in ("lat", "fv", "mv")}
        ln_loaded = sem("ln_loaded")
        stored = sem("stored")
        dve_step = sem("dve_step")
        act_step = sem("act_step")
        sq_ready = sem("sq_ready")
        rstd_ready = sem("rstd_ready")
        nz_ready = sem("nz_ready")
        lse_ready = sem("lse_ready")
        lat_ready = sem("lat_ready")
        logf_ready = sem("logf_ready")
        qrope_ready = sem("qrope_ready")
        prep_ready = sem("prep_ready")
        max_ready = sem("max_ready")
        exp_ready = sem("exp_ready")
        norm_ready = sem("norm_ready")
        lnv_ready = sem("lnv_ready")
        rstd1_ready = sem("rstd1_ready")
        x1_ready = sem("x1_ready")
        y_out = sem("y_out")
        x1_stored = sem("x1_stored")
        router_loaded = sem("router_loaded")
        ln2_loaded = sem("ln2_loaded")
        z_ready = sem("z_ready")
        ez_ready = sem("ez_ready")
        mask_ready = sem("mask_ready")
        count_ready = sem("count_ready")
        flag_ready = sem("flag_ready")
        hidden_ready = sem("hidden_ready")
        gate_up_loaded = [sem(f"gate_up_loaded{i}") for i in range(4)]
        down_loaded = [sem(f"down_loaded{i}") for i in range(4)]
        onehot_built = sem("onehot_built")
        slots_done = sem("slots_done")
        idx_ready = sem("idx_ready")
        column_copied = sem("column_copied")
        gathers_started = sem("gathers_started")
        xg_loaded = [sem(f"xg_loaded{i}") for i in range(2)]
        xg_turned = sem("xg_turned")
        xgT_ready = sem("xgT_ready")
        gate_up_done = sem("gate_up_done")
        silu_ready = sem("silu_ready")
        hid_ready = sem("hid_ready")
        down_done = sem("down_done")
        down_free = sem("down_free")
        rows_stored = [sem(f"rows_stored{i}") for i in range(2)]
        all_written = sem("all_written")
        row_idx_ready = sem("row_idx_ready")
        rows_added = sem("rows_added")
        zero_row_stored = sem("zero_row_stored")
        overflow_step = sem("overflow_step")
        rows_gathered = [sem(f"rows_gathered{i}") for i in range(TT * TOPK)]
        out_ready = sem("out_ready")

        d_of = {
            "lat": a["w_in"][0], "in": a["w_in"][0], "mem_k": a["w_mem_k"][0], "mem_v": a["w_mem_v"][0],
            "br_mla": a["w_br_mla"][0], "br_fox": a["w_br_fox"][0], "br_mem": a["w_br_mem"][0], "out": a["w_out"][0],
        }

        def rowblocks(m, k0, nk, c0, n):
            return m[k0 * P:(k0 + nk) * P, c0:c0 + n].rearrange("(k p) n -> p k n", p=P)

        def unit_stage(n):
            return U[n][4], U[n][5] // P

        def rounds(eng, body):
            body(0)
            eng.wait_ge(flag_ready, 1)
            most = eng.value_load(flag_i[0:1, 0:1], min_val=0, max_val=T)
            for r in range(1, ROUNDS):
                with eng.If(most > r * CAP):
                    body(r)

        block = ctx.enter_context(nc.Block())

        @block.sync
        def _(sp):
            def w_load(n):
                name, k0, c0, w = WU[n] if len(WU[n]) == 4 else WU[n] + (0, 0, 0)
                if n >= NW:
                    ring = last_use[n - NW][0]
                    sp.wait_ge(done[ring], done_at(*last_use[n - NW]))
                s = n % NW
                if n >= first_of["s_gate"]:
                    dst, src = ((sh_gate, rowblocks(a["w_s_gate"][0], 0, KD, 0, FE)), (sh_upw, rowblocks(a["w_s_up"][0], 0, KD, 0, FE)),
                                (sh_down, rowblocks(a["w_s_down"][0], 0, 2, 0, D)))[n - first_of["s_gate"]]
                    sp.dma_start(dst, src).then_inc(w_loaded[s], 16)
                    return
                sp.dma_start(wring[:, s, :, 0:w], rowblocks(d_of[name], k0, 4, c0, w)).then_inc(w_loaded[s], 16)
                if name == "lat":
                    sp.dma_start(wring[:, s, :, 416:424],
                                 rowblocks(d_of[name], k0, 4, OFF["fl"], 8)).then_inc(w_loaded[s], 16)

            def load_expert(r, i, q):
                e = i * 4 + q
                if r or not isinstance(i, int):
                    sp.wait_ge(gate_up_done, E * r + e - 3)
                sp.dma_start(ew_gate[q], w_eg[bass.ds(e, 1)].rearrange("e (p k) f -> p (e k) f", p=P)).then_inc(gate_up_loaded[q], 16)
                sp.dma_start(ew_up[q], w_eu[bass.ds(e, 1)].rearrange("e (p k) f -> p (e k) f", p=P)).then_inc(gate_up_loaded[q], 16)
                if r or not isinstance(i, int):
                    sp.wait_ge(down_done, 2 * (E * r + e - 3))
                sp.dma_start(ew_down[q], w_ed[bass.ds(e, 1)].rearrange("e (m p) n -> p (e m) n", p=P)).then_inc(down_loaded[q], 16)

            w_eg, w_eu, w_ed = a["w_e_gate"][0], a["w_e_up"][0], a["w_e_down"][0]
            xs = [a["x_prompt"][0, 0:P], a["x_prompt"][0, P:2 * P], a["x_sample"].rearrange("b s d -> (b s) d")]
            sp.dma_start(cst[:, :], a["consts"]).then_inc(cst_loaded, 16)
            sp.dma_start(y_dram[E * CAP:E * CAP + 1, :], a["zero_row"]).then_inc(zero_row_stored, 16)
            for j in range(TT):
                sp.dma_start(x_sb[:, j, :], xs[j]).then_inc(x_loaded[j], 16)
            w_load(0)
            w_load(1)
            for t, v, n in ((gq_b, "q_norm_g", 256), (gkv_b, "kv_norm_g", 128), (b_f_b, "b_f", 8)):
                sp.dma_start(t, a[v].to_broadcast([P, n])).then_inc(vec_loaded, 16)
            for j in range(2):
                sp.dma_start(mem_sb[:, j, :], a["mem_prompt"][0, j * P:(j + 1) * P]).then_inc(mem_loaded[j], 16)
            sp.dma_start(w_kv, a["w_kv_up"][0]).then_inc(up_loaded, 16)
            w_load(2)
            w_load(3)
            sp.dma_start(w_q, rowblocks(a["w_q_up"][0], 0, 2, 0, 768)).then_inc(up_loaded, 16)
            for n in range(4, 14):
                w_load(n)
            for n in range(14, 14 + NW):
                w_load(n)

            def wait_unit(kind, b, ring):
                n = next(i for i, u in enumerate(U) if u[:3] == (kind, "s", b))
                sp.wait_ge(done[ring], done_at("V", "o", n))
            sp.wait_ge(done["T"], done_at("T", "mk", 1))
            sp.wait_ge(done["P"], done_at("P", "mv", 1))
            sp.wait_ge(stored, 16 * E_STORES)
            sp.wait_ge(free["V"], done_at("V", "c", "p"))
            sp.dma_start(lfc_raw, a["cache_fox_logf"][0].rearrange("b (t p) h -> p (b t) h", p=P)).then_inc(logf_loaded, 16)
            for b in range(NB):
                if b >= 2:
                    wait_unit("mla", b - 2, "V")
                sp.dma_start(latc[b % 2], a["cache_mla_latent"][0, b].rearrange("(t p) c -> p t c", p=P)).then_inc(vcache["lat"][b % 2], 16)
                sp.dma_start(krc[b % 2], a["cache_mla_krope"][0, b].rearrange("(t p) c -> p t c", p=P)).then_inc(vcache["lat"][b % 2], 16)
                if b >= 1:
                    sp.wait_ge(done["T"], done_at("T", "cfk", b - 1, 1))
                sp.dma_start(fkc, a["cache_fox_k"][0, b].rearrange("(t p) h c -> p t (h c)", p=P)).then_inc(kcache["fk"], 16)
                if b >= 2:
                    wait_unit("fox", b - 2, "V")
                sp.dma_start(fvc[b % 2], a["cache_fox_v"][0, b].rearrange("(t p) h c -> p t (h c)", p=P)).then_inc(vcache["fv"][b % 2], 16)
                if b >= 1:
                    sp.wait_ge(done["T"], done_at("T", "cmk", b - 1, 1))
                sp.dma_start(mkc, a["cache_mem_k"][0, b].rearrange("(t p) h c -> p t (h c)", p=P)).then_inc(kcache["mk"], 16)
                if b >= 2:
                    wait_unit("mem", b - 2, "V")
                sp.dma_start(mvc[b % 2], a["cache_mem_v"][0, b].rearrange("(t p) h c -> p t (h c)", p=P)).then_inc(vcache["mv"][b % 2], 16)
            for n in range(14 + NW, len(WU)):
                w_load(n)
                if n in (23, 26, 29, 32):
                    load_expert(0, 0, (n - 23) // 3)
                if n == 22:
                    sp.wait_ge(done["V"], done_at("V", "b", 0, 0, 0))
                    sp.dma_start(lngb[:, 0:D], a["ln1_g"].to_broadcast([P, D])).then_inc(ln_loaded, 16)
                    sp.dma_start(lngb[:, D:2 * D], a["ln1_b"].to_broadcast([P, D])).then_inc(ln_loaded, 16)
            sp.wait_ge(free["T"], done_at("T", "y", 2, 1))
            sp.wait_ge(done["T"], done_at("T", "y", 2, 1))
            sp.dma_start(w_rt, rowblocks(a["w_router"][0], 0, KD, 0, E)).then_inc(router_loaded, 16)
            sp.dma_start(rb_b, a["router_bias"].to_broadcast([P, E])).then_inc(router_loaded, 16)
            sp.wait_ge(x1_ready, TT)
            sp.dma_start(x1_dram.rearrange("(j p) d -> p j d", p=P), x_sb).then_inc(x1_stored, 16)
            sp.dma_start(lngb[:, 0:D], a["ln2_g"].to_broadcast([P, D])).then_inc(ln2_loaded, 16)
            sp.dma_start(lngb[:, D:2 * D], a["ln2_b"].to_broadcast([P, D])).then_inc(ln2_loaded, 16)

            def expert_round(r):
                if r:
                    sp.wait_ge(rows_added, TT * TOPK * r)
                    for q in range(4):
                        load_expert(r, 0, q)
                with sp.Fori(1, E // 4) as i:
                    for q in range(4):
                        load_expert(r, i, q)
            rounds(sp, expert_round)
            sp.wait_ge(out_ready, TT)
            sp.dma_start(outs["y_prompt"][0].rearrange("(j p) d -> p j d", p=P), x_sb[:, 0:2, :]).then_inc(y_out, 16)
            sp.dma_start(outs["y_sample"].rearrange("b s d -> (b s) d"), x_sb[:, 2, :]).then_inc(y_out, 16)
            sp.wait_ge(y_out, 32)

        def store_pair(eng, pn, sn, src):
            eng.dma_start(flat_out("p_" + pn, 2), src[:, 0:2, :]).then_inc(stored, 16)
            eng.dma_start(flat_out("s_" + sn, 1), src[:, 2:3, :]).then_inc(stored, 16)

        def flat_out(name, nj):
            o = outs[name]
            nd = len(o.shape)
            if nd == 4:
                return o.rearrange("o b s c -> (o b s) c").rearrange("(j p) c -> p j c", p=P)
            return o.rearrange("o b s h c -> (o b s) (h c)").rearrange("(j p) c -> p j c", p=P)

        @block.gpsimd
        def _(pool):
            pool.wait_ge(lat_ready, 1)
            store_pair(pool, "mla_latent", "mla_latent", latn)
            store_pair(pool, "mla_krope", "mla_krope", kr_rot)
            pool.wait_ge(logf_ready, 1)
            store_pair(pool, "fox_logf", "fox_logf", lf_new)
            pool.wait_ge(free["P"], done_at("P", "fk", 2))
            store_pair(pool, "fox_k", "fox_k", fk_tok)
            pool.wait_ge(free["P"], done_at("P", "fv", 2))
            store_pair(pool, "fox_v", "fox_v", fv_tok)
            pool.wait_ge(free["P"], done_at("P", "mk", 1))
            pool.dma_start(flat_out("p_mem_k", 2), mk_tok).then_inc(stored, 16)
            pool.wait_ge(free["P"], done_at("P", "mv", 1))
            pool.dma_start(flat_out("p_mem_v", 2), mv_tok).then_inc(stored, 16)
            pool.wait_ge(stored, 16 * E_STORES)
            pool.wait_ge(x1_stored, 16)

            def gather(r, e, par):
                pool.wait_ge(idx_ready, (E + 2) * r + e + 1)
                pool.sem_inc(gathers_started, 1)
                pool.indirect_dma_start(xg[par][0:CAP, :], None, x1_dram, bass.IndirectOffsetOnAxis(ap=idx[0:CAP, par:par + 1], axis=0))\
                    .then_inc(xg_loaded[par], 16)

            def expert_round(r):
                gather(r, 0, 0)
                gather(r, 1, 1)
                with pool.Fori(0, E // 2) as i:
                    gather(r, i * 2 + 2, 0)
                    gather(r, i * 2 + 3, 1)
                for par in range(2):
                    pool.wait_ge(xg_loaded[par], 16 * (E // 2 + 1) * (r + 1))
                pool.wait_ge(all_written, r + 1)
                pool.wait_ge(zero_row_stored, 16)
                pool.wait_ge(row_idx_ready, r + 1)
                for n in range(TT * TOPK):
                    pool.indirect_dma_start(gathered_rows[:, n, :], None, y_dram,
                                            bass.IndirectOffsetOnAxis(ap=row_idx[:, n:n + 1], axis=0)).then_inc(rows_gathered[n], 16)
            rounds(pool, expert_round)

        @block.tensor
        def _(pe):
            mm = nc.tensor.matmul

            def bank(st):
                n = pos_in[st]
                if n >= 2:
                    pe.wait_ge(free[st[0]], n - 1)
                return ps[st[0]][n % 2]

            def w_wait(n):
                s = n % NW
                per = [32 if WU[m][0] == "lat" else 16 for m in range(n + 1) if m % NW == s]
                pe.wait_ge(w_loaded[s], sum(per))
                return wring[:, s]

            def tr(out, in_, n):
                return nc.tensor.transpose(out, in_, ident[0:n, 0:n])

            def tok_major(st, first, src, j, w):
                out = bank(st)
                for k in range(KD):
                    if k % 4 == 0:
                        slot = w_wait(first + k // 4)
                    last = mm(out[:, 0:w], src[:, k, j * P:(j + 1) * P], slot[:, k % 4, 0:w], start=(k == 0), stop=(k == KD - 1))
                last.then_inc(done["P"], 1)

            def feat_major(st, first, m):
                out = bank(st)
                for k in range(KD):
                    if k % 4 == 0:
                        slot = w_wait(first + k // 4)
                    last = mm(out[:, 0:T], slot[:, k % 4, m * P:(m + 1) * P], xT[:, k, :], start=(k == 0), stop=(k == KD - 1))
                last.then_inc(done["P"], 1)

            def scores(n):
                kind, g, i, q, rows, keys = U[n]
                pe.wait_ge(prep_ready, n + 1)
                out = bank(("S", n))
                if g == "p":
                    qs = slice(q * P, (q + 1) * P)
                    if kind == "mla":
                        mm(out[:, 0:keys], qabsP[:, i, qs], latT[:, 0:keys], start=True, stop=False)
                        mm(out[:, 0:keys], qrP[0:RD, i, qs], krT[0:RD, 0:keys], start=False, stop=False)
                        last = mm(out[:, keys - P:keys], ident, cc("chunk"), start=False, stop=True)
                    elif kind == "fox":
                        h0 = (i % 2) * 64
                        mm(out[:, 0:keys], fqT[h0:h0 + 64, i // 2, qs], fkT[h0:h0 + 64, i // 2, 0:keys], start=True, stop=False)
                        mm(out[:, 0:keys], LH[:, qs], FR[:, 0:keys], start=False, stop=False)
                        last = mm(out[:, keys - P:keys], ident, cc("causal"), start=False, stop=True)
                    else:
                        last = mm(out[:, 0:keys], mqT[:, i, qs], mkT[:, i, :], start=True, stop=True)
                elif kind == "mla":
                    mm(out[:, 0:PAST], qabsS[:, i, :], latTc, start=True, stop=False)
                    mm(out[:, 0:PAST], qrS[0:RD, i, :], krTc[0:RD, :], start=False, stop=False)
                    mm(out[:, PAST:keys], qabsS[:, i, :], latT[:, 256:T], start=False, stop=False)
                    mm(out[:, PAST:keys], qrS[0:RD, i, :], krT[0:RD, 256:T], start=False, stop=False)
                    w0 = (7 - i) * NQ
                    last = mm(out[:, PAST:keys], ident, cc("wmla")[:, w0:w0 + P], start=False, stop=True)
                elif kind == "fox":
                    for m in range(4):
                        mm(out[:, 0:PAST], qbd_fox[:, m * P:(m + 1) * P], fkTc[:, m, :], start=(m == 0), stop=False)
                    for m in range(4):
                        mm(out[:, PAST:keys], qbd_fox[:, m * P:(m + 1) * P], fkT[:, m, 256:T], start=False, stop=False)
                    mm(out[:, 0:keys], LH[:, 0:P], FR[:, :], start=False, stop=False)
                    w0 = (7 - i) * NQ
                    last = mm(out[:, PAST:keys], ident, cc("wfox")[:, w0:w0 + P], start=False, stop=True)
                else:
                    for m in range(HM):
                        last = mm(out[0:64, 0:keys], qbd_mem[:, m * 64:(m + 1) * 64], mkTc[:, m, :], start=(m == 0), stop=(m == HM - 1))
                last.then_inc(done["S"], 1)

            def values(n):
                kind, g, i, q, rows, keys = U[n]
                pe.wait_ge(free["T"], done_at("T", "p", n))
                out = bank(("V", "o", n))
                pt = pT[n % 2]
                nk = keys // P
                if kind == "mla":
                    for t in range(nk):
                        if g == "p":
                            v = latn[:, t, :]
                        else:
                            v = latc[i % 2][:, t, :] if t < 2 else latn[:, 2, :]
                        last = mm(out[:, 0:P], v, pt[:, t * P:(t + 1) * P], start=(t == 0), stop=(t == nk - 1))
                elif kind == "fox" and g == "p":
                    h0 = (i % 2) * 64
                    for t in range(nk):
                        last = mm(out[h0:h0 + 64, 0:P], fv_tok[:, t, i * 64:(i + 1) * 64], pt[:, t * P:(t + 1) * P],
                                  start=(t == 0), stop=(t == nk - 1))
                elif kind == "fox":
                    pe.wait_ge(vcache["fv"][i % 2], 16 * (i // 2 + 1))
                    for m in range(4):
                        for t in range(nk):
                            v = fvc[i % 2][:, t, m * P:(m + 1) * P] if t < 2 else fv_tok[:, 2, m * P:(m + 1) * P]
                            last = mm(out[:, m * 32:(m + 1) * 32], v, pt[:, t * P + m * 32:t * P + (m + 1) * 32],
                                      start=(t == 0), stop=(t == nk - 1))
                elif g == "p":
                    for t in range(nk):
                        last = mm(out[:, 0:P], mv_tok[:, t, i * P:(i + 1) * P], pt[:, t * P:(t + 1) * P],
                                  start=(t == 0), stop=(t == nk - 1))
                else:
                    pe.wait_ge(vcache["mv"][i % 2], 16 * (i // 2 + 1))
                    for m in range(HM):
                        for t in range(nk):
                            last = mm(out[:, m * NQ:(m + 1) * NQ], mvc[i % 2][:, t, m * P:(m + 1) * P],
                                      pt[:, t * P + m * NQ:t * P + (m + 1) * NQ], start=(t == 0), stop=(t == nk - 1))
                last.then_inc(done["V"], 1)

            pe.wait_ge(cst_loaded, 16)
            for st in PLAN:
                ring, key = st[0], st[1:]
                if ring == "T":
                    if key[0] == "x":
                        _, j, half = key
                        pe.wait_ge(x_loaded[j], 16)
                        out = bank(st)
                        for k in range(4):
                            kk = half * 4 + k
                            last = tr(out[:, k * P:(k + 1) * P], x_sb[:, j, kk * P:(kk + 1) * P], P)
                    elif key[0] == "mem":
                        _, j, half = key
                        pe.wait_ge(mem_loaded[j], 16)
                        out = bank(st)
                        for k in range(4):
                            kk = half * 4 + k
                            last = tr(out[:, k * P:(k + 1) * P], mem_sb[:, j, kk * P:(kk + 1) * P], P)
                    elif key[0] == "uk":
                        pe.wait_ge(up_loaded, 32)
                        out = bank(st)
                        for k in range(4):
                            h = key[1] * 4 + k
                            last = tr(out[0:64, k * P:(k + 1) * P], w_kv[:, h * P:h * P + 64], P)
                    elif key[0] == "lat":
                        j = key[1]
                        pe.wait_ge(lat_ready, 1)
                        out = bank(st)
                        tr(out[:, 0:P], qn[:, j, 0:P], P)
                        tr(out[:, P:2 * P], qn[:, j, P:2 * P], P)
                        tr(out[:, 2 * P:3 * P], latn[:, j, :], P)
                        last = tr(out[0:RD, 3 * P:4 * P], kr_rot[:, j, :], P)
                    elif key[0] == "qr":
                        _, j, half = key
                        pe.wait_ge(qrope_ready, j + 1)
                        out = bank(st)
                        for k in range(4):
                            h = half * 4 + k
                            last = tr(out[0:RD, k * P:(k + 1) * P], qr_rot[:, j, h * RD:(h + 1) * RD], P)
                    elif key[0] == "fk":
                        j = key[1]
                        pe.wait_ge(free["P"], done_at("P", "fk", j))
                        out = bank(st)
                        for m in range(4):
                            last = tr(out[:, m * P:(m + 1) * P], fk_tok[:, j, m * P:(m + 1) * P], P)
                    elif key[0] == "mk":
                        j = key[1]
                        pe.wait_ge(free["P"], done_at("P", "mk", j))
                        out = bank(st)
                        for m in range(4):
                            last = tr(out[:, m * P:(m + 1) * P], mk_tok[:, j, m * P:(m + 1) * P], P)
                    elif key[0] == "clat":
                        b = key[1]
                        pe.wait_ge(vcache["lat"][b % 2], 32 * (b // 2 + 1))
                        out = bank(st)
                        for t in range(2):
                            tr(out[:, t * P:(t + 1) * P], latc[b % 2][:, t, :], P)
                            last = tr(out[0:RD, (2 + t) * P:(3 + t) * P], krc[b % 2][:, t, :], P)
                    elif key[0] in ("cfk", "cmk"):
                        _, b, t = key
                        src = fkc if key[0] == "cfk" else mkc
                        pe.wait_ge(kcache[key[0][1:]], 16 * (b + 1))
                        out = bank(st)
                        for m in range(4):
                            last = tr(out[:, m * P:(m + 1) * P], src[:, t, m * P:(m + 1) * P], P)
                    elif key[0] == "p":
                        n = key[1]
                        rows, nk = unit_stage(n)
                        pe.wait_ge(norm_ready, n + 1)
                        out = bank(st)
                        for t in range(nk):
                            last = tr(out[:, t * P:t * P + rows], prob[n % 3][0:rows, t * P:(t + 1) * P], rows)
                    elif key[0] == "y":
                        _, j, half = key
                        pe.wait_ge(free["V"], done_at("V", "b", 2, 1, 2))
                        out = bank(st)
                        for k in range(4):
                            kk = half * 4 + k
                            last = tr(out[:, k * P:(k + 1) * P], y[:, j, kk * P:(kk + 1) * P], P)
                    elif key[0] == "x1":
                        _, j, half = key
                        pe.wait_ge(x1_ready, j + 1)
                        out = bank(st)
                        for k in range(4):
                            kk = half * 4 + k
                            last = tr(out[:, k * P:(k + 1) * P], x_sb[:, j, kk * P:(kk + 1) * P], P)
                    last.then_inc(done["T"], 1)
                elif ring == "P":
                    if key[0] == "lat":
                        pe.wait_ge(free["T"], done_at("T", "x", key[1], 1))
                        tok_major(st, first_of["lat"], xT, key[1], 424)
                    elif key[0] in ("fk", "fv"):
                        tok_major(st, first_of[key[0]], xT, key[1], 512)
                    elif key[0] in ("mk", "mv"):
                        pe.wait_ge(free["T"], done_at("T", "mem", 1, 1))
                        tok_major(st, first_of[key[0]], memT, key[1], 512)
                    elif key[0] in ("fq", "mq"):
                        feat_major(st, first_of[key[0]], key[1])
                    elif key[0] == "qr":
                        j = key[1]
                        pe.wait_ge(free["T"], done_at("T", "lat", j))
                        pe.wait_ge(up_loaded, 32)
                        out = bank(st)
                        for k in range(2):
                            wv = w_q[:, k, :].rearrange("p (h c) -> p h c", h=H)[:, :, ND:ND + RD]
                            last = mm(out[:, 0:256], qnT[:, k, j * P:(j + 1) * P], wv, start=(k == 0), stop=(k == 1))
                        last.then_inc(done["P"], 1)
                    elif key[0] == "qn":
                        h = key[1]
                        out = bank(st)
                        for k in range(2):
                            last = mm(out[0:64, 0:T], w_q[:, k, h * 96:h * 96 + 64], qnT[:, k, :], start=(k == 0), stop=(k == 1))
                        last.then_inc(done["P"], 1)
                    elif key[0] == "qa":
                        h = key[1]
                        pe.wait_ge(free["P"], done_at("P", "qn", h))
                        pe.wait_ge(free["T"], done_at("T", "uk", 1))
                        out = bank(st)
                        mm(out[:, 0:T], wukT[0:64, h, :], qn_up[0:64, h % 2, :], start=True, stop=True).then_inc(done["P"], 1)
                    elif key[0] == "g":
                        _, br, cb, j = key
                        tok_major(st, first_of["g"] + (br * 2 + cb) * 3, xT, j, 512)
                    elif key[0] == "sh":
                        m = key[1]
                        pe.wait_ge(free["T"], done_at("T", "x1", 2, 1))
                        w_wait(first_of["s_gate"] + m // 2)
                        out = bank(st)
                        wv = (sh_gate, sh_upw)[m // 2]
                        for k in range(KD):
                            last = mm(out[:, 0:T], wv[:, k, (m % 2) * P:(m % 2 + 1) * P], xT[:, k, :], start=(k == 0), stop=(k == KD - 1))
                        last.then_inc(done["P"], 1)
                elif ring == "S":
                    n = key[0]
                    scores(n)
                elif ring == "V":
                    if key[0] == "c":
                        out = bank(st)
                        if key[1] == "p":
                            pe.wait_ge(logf_ready, 1)
                            mm(out[0:40, 0:256], LFn[:, 0, :], cst[:, CST["tri"][0]:CST["tri"][0] + 256], start=True, stop=False)
                            last = mm(out[0:40, P:256], LFn[:, 1, :], cc("tri"), start=False, stop=True)
                        else:
                            b = key[1]
                            n = next(i for i, u in enumerate(U) if u[:3] == ("fox", "s", b))
                            pe.wait_ge(prep_ready, n)
                            t0 = CST["tri"][0]
                            mm(out[0:40, 0:T], LFc[b % 2][:, 0, :], cst[:, t0:t0 + T], start=True, stop=False)
                            mm(out[0:40, P:T], LFc[b % 2][:, 1, :], cst[:, t0:t0 + 256], start=False, stop=False)
                            last = mm(out[0:40, 256:T], LFn[:, 2, :], cc("blk"), start=False, stop=True)
                        last.then_inc(done["V"], 1)
                    elif key[0] == "o":
                        values(key[1])
                    elif key[0] == "ov":
                        kind, g, i, q, rows, keys = U[key[1]]
                        pe.wait_ge(free["V"], done_at("V", "o", key[1]))
                        out = bank(st)
                        if g == "p":
                            h0 = (i % 2) * 64
                            last = mm(out[h0:h0 + 64, 0:P], w_kv[:, i * P + 64:(i + 1) * P], olat[key[1] % 2], start=True, stop=True)
                        else:
                            for h in range(H):
                                h0 = (h % 2) * 64
                                last = mm(out[h0:h0 + 64, (h // 2) * NQ:(h // 2 + 1) * NQ], w_kv[:, h * P + 64:(h + 1) * P],
                                          olat[key[1] % 2][:, h * NQ:(h + 1) * NQ], start=True, stop=True)
                        last.then_inc(done["V"], 1)
                    elif key[0] == "b":
                        _, br, cb, j = key
                        pe.wait_ge(free["V"], done_at("V", "o", len(U) - 1))
                        slot = w_wait(first_of["g"] + (br * 2 + cb) * 3 + 2)
                        out = bank(st)
                        for k in range(4):
                            last = mm(out[:, :], oT[:, br, k, j * P:(j + 1) * P], slot[:, k, :], start=(k == 0), stop=(k == 3))
                        last.then_inc(done["V"], 1)
                    elif key[0] == "out":
                        _, j, half = key
                        pe.wait_ge(free["T"], done_at("T", "y", j, 1))
                        out = bank(st)
                        for k in range(KD):
                            if k % 4 == 0:
                                slot = w_wait(first_of["out"] + half * 2 + k // 4)
                            last = mm(out[:, :], yT[:, k, j * P:(j + 1) * P], slot[:, k % 4, :], start=(k == 0), stop=(k == KD - 1))
                        last.then_inc(done["V"], 1)
                    elif key[0] == "router":
                        j = key[1]
                        pe.wait_ge(free["T"], done_at("T", "x1", 2, 1))
                        pe.wait_ge(router_loaded, 32)
                        out = bank(st)
                        for k in range(KD):
                            last = mm(out[:, 0:E], xT[:, k, j * P:(j + 1) * P], w_rt[:, k, :], start=(k == 0), stop=(k == KD - 1))
                        last.then_inc(done["V"], 1)
                    elif key[0] == "pos":
                        j = key[1]
                        pe.wait_ge(mask_ready, 1)
                        out = bank(st)
                        for jj in range(j):
                            mm(out[:, 0:E], cc("ones")[:, 0:P], mask[:, jj, :], start=(jj == 0), stop=False)
                        mm(out[:, 0:E], cc("strict"), mask[:, j, :], start=(j == 0), stop=True).then_inc(done["V"], 1)
                    elif key[0] == "flag":
                        pe.wait_ge(count_ready, 1)
                        tr(bank(st)[0:1, 0:P], cmax, P).then_inc(done["V"], 1)
                    elif key[0] == "shd":
                        _, j, half = key
                        pe.wait_ge(hidden_ready, 1)
                        w_wait(first_of["s_down"])
                        out = bank(st)
                        for m in range(2):
                            last = mm(out[:, :], sh_sil[:, m, j * P:(j + 1) * P], sh_down[:, m, half * 512:(half + 1) * 512],
                                      start=(m == 0), stop=(m == 1))
                        last.then_inc(done["V"], 1)

            def slot_tokens(r, e, par):
                pe.wait_ge(onehot_built, (E + 3) * r + e + 1)
                for j in range(TT):
                    last = mm(ps["S"][par][0:CAP, 0:2], onehot[par][:, j, :], pcol[par][:, j, 0:2], start=(j == 0), stop=(j == TT - 1))
                last.then_inc(slots_done, 1)

            def turn(r, e, count, par):
                pe.wait_ge(xg_loaded[par], 16 * ((E // 2 + 1) * r + count + 1))
                xv = xg[par][0:CAP, :].rearrange("c (d k) -> c k d", k=KD)
                for half in range(2):
                    for k in range(4):
                        last = nc.tensor.transpose(ps["T"][half][:, k * CAP:(k + 1) * CAP], xv[:, half * 4 + k, :], ident[0:CAP, 0:CAP])
                    last.then_inc(xg_turned, 1)

            def expert(r, i, q):
                e, par = i * 4 + q, q % 2
                slot_tokens(r, e + 2, par)
                pe.wait_ge(gate_up_loaded[q], 32 * ((E // 4) * r + i + 1))
                pe.wait_ge(xgT_ready, 2 * ((E + 1) * r + e + 1))
                pe.wait_ge(hid_ready, E * r + e + 1)
                out = ps["P"][par]
                for m in range(4):
                    wv = (ew_gate, ew_up)[m // 2][q]
                    for k in range(KD):
                        last = mm(out[:, m * CAP:(m + 1) * CAP], wv[:, k, (m % 2) * P:(m % 2 + 1) * P], xgT[par][:, k, :],
                                  start=(k == 0), stop=(k == KD - 1))
                last.then_inc(gate_up_done, 1)
                turn(r, e + 1, i * 2 + (q + 1) // 2, 1 - par)
                pe.wait_ge(down_loaded[q], 16 * ((E // 4) * r + i + 1))
                pe.wait_ge(hid_ready, E * r + e + 3)
                pe.wait_ge(down_free, 2 * (E * r + e + 1))
                for half in range(2):
                    for m in range(2):
                        last = mm(ps["V"][half][0:CAP, :], hid[par][:, m, :], ew_down[q][:, m, half * 512:(half + 1) * 512],
                                  start=(m == 0), stop=(m == 1))
                    last.then_inc(down_done, 1)

            def expert_round(r):
                slot_tokens(r, 0, 0)
                slot_tokens(r, 1, 1)
                turn(r, 0, 0, 0)
                with pe.Fori(0, E // 4) as i:
                    for q in range(4):
                        expert(r, i, q)
            for ring in "PTV":
                pe.wait_ge(free[ring], count[ring])
            rounds(pe, expert_round)

        @block.scalar
        def _(act):
            chain = [0]

            def link(ins):
                chain[0] += 1
                ins.then_inc(act_step, 1)
                act.wait_ge(act_step, chain[0])

            fn = nc.scalar.activation
            act.wait_ge(cst_loaded, 16)
            one = cc("ones")[:, 0:1]
            eps = cc("eps")
            for st in PLAN:
                ring, key = st[0], st[1:]
                if ring == "P":
                    act.wait_ge(done["P"], done_at(*st))
                    src = ps["P"][pos_in[st] % 2]
                    if key[0] == "lat":
                        last = fn(lat_raw[:, key[1], :], src[:, 0:424], ACT.Copy)
                    elif key[0] == "fk":
                        last = fn(fk_tok[:, key[1], :], src[:, :], ACT.Copy)
                    elif key[0] == "fv":
                        last = fn(fv_tok[:, key[1], :], src[:, :], ACT.Copy)
                    elif key[0] == "fq":
                        last = fn(fqT[:, key[1], :], src[:, 0:T], ACT.Copy, scale=FOX_SCALE)
                    elif key[0] == "mq":
                        last = fn(mqT[:, key[1], :], src[:, 0:T], ACT.Copy, scale=MEM_SCALE)
                    elif key[0] == "mk":
                        last = fn(mk_tok[:, key[1], :], src[:, :], ACT.Copy)
                    elif key[0] == "mv":
                        last = fn(mv_tok[:, key[1], :], src[:, :], ACT.Copy)
                    elif key[0] == "qr":
                        last = fn(qr_tok[:, key[1], :], src[:, 0:256], ACT.Copy, scale=MLA_SCALE)
                    elif key[0] == "qn":
                        h = key[1]
                        if h >= 2:
                            act.wait_ge(done["P"], done_at("P", "qa", h - 2))
                        last = fn(qn_up[0:64, h % 2, :], src[0:64, 0:T], ACT.Copy)
                    elif key[0] == "qa":
                        h = key[1]
                        fn(qabsP[:, h, :], src[:, 0:256], ACT.Copy, scale=MLA_SCALE)
                        last = fn(qabsS.rearrange("p b (h q) -> p b h q", h=H)[:, :, h, :],
                                  src[:, 256:T].rearrange("p (b q) -> p b q", b=NB), ACT.Copy, scale=MLA_SCALE)
                    elif key[0] == "g":
                        n = (key[1] * 2 + key[2]) * TT + key[3]
                        if n >= 2:
                            pb = [s for s in PLAN if s[0:2] == ("V", "b")][n - 2]
                            act.wait_ge(free["V"], done_at(*pb))
                        else:
                            act.wait_ge(free["V"], done_at("V", "o", len(U) - 1))
                        last = fn(egate[n % 2], src[:, :], ACT.Exp, scale=-1.0)
                    elif key[0] == "sh":
                        m = key[1]
                        if m < 2:
                            last = fn(sh_sil[:, m, :], src[:, 0:T], ACT.Silu)
                        else:
                            last = fn(sh_up[:, m - 2, :], src[:, 0:T], ACT.Copy)
                    last.then_inc(free["P"], 1)
                elif ring == "rms":
                    act.wait_ge(sq_ready, 1)
                    link(fn(rst[:, 0:3], ssq[:, 0:3], ACT.Ln, bias=eps, scale=1.0 / QL))
                    link(fn(rst[:, 3:6], ssq[:, 3:6], ACT.Ln, bias=eps, scale=1.0 / KVL))
                    fn(rst[:, :], rst[:, :], ACT.Exp, scale=-0.5).then_inc(rstd_ready, 1)
                    act.wait_ge(nz_ready, 1)
                    link(fn(lft[:, 2, :], lft[:, 1, :], ACT.Exp))
                    fn(lft[:, 3, :], lft[:, 2, :], ACT.Ln, bias=one).then_inc(lse_ready, 1)
                elif ring == "S":
                    n = key[0]
                    rows, nk = unit_stage(n)
                    act.wait_ge(max_ready, n + 1)
                    if n >= 3:
                        act.wait_ge(done["T"], done_at("T", "p", n - 3))
                    fn(prob[n % 3][0:rows, 0:nk * P], ps["S"][n % 2][0:rows, 0:nk * P], ACT.Exp, bias=mx[0:rows, n:n + 1],
                       accum_out=sm[0:rows, n:n + 1]).then_inc(exp_ready, 1)
                elif ring == "ln1":
                    for j in range(TT):
                        act.wait_ge(lnv_ready, j + 1)
                        link(fn(rst[:, j:j + 1], rt[:, 0, 2 * j + 1:2 * j + 2], ACT.Ln, bias=eps))
                        fn(rst[:, j:j + 1], rst[:, j:j + 1], ACT.Exp, scale=-0.5).then_inc(rstd1_ready, 1)
                elif st == ("V", "router", 2):
                    act.wait_ge(z_ready, 1)
                    fn(sel, sc, ACT.Exp, scale=-1.0).then_inc(ez_ready, 1)

            def expert(r, i, q):
                e, par = i * 4 + q, q % 2
                act.wait_ge(gate_up_done, E * r + e + 1)
                fn(sil[par], ps["P"][par][:, 0:2 * CAP].rearrange("p (m c) -> p m c", m=2), ACT.Silu).then_inc(silu_ready, 1)
                act.wait_ge(rows_stored[par], 16 * ((E // 2) * r + i * 2 + q // 2 + 1))
                for half in range(2):
                    act.wait_ge(down_done, 2 * (E * r + e) + half + 1)
                    fn(yo[par][0:CAP, half * 512:(half + 1) * 512], ps["V"][half][0:CAP, :], ACT.Copy, scale=gslot[0:CAP, q:q + 1])\
                        .then_inc(down_free, 1)
                act.wait_ge(down_free, 2 * (E * r + e + 2))
                act.dma_start(y_dram[bass.ds(e * CAP, CAP), :], yo[par][0:CAP, :]).then_inc(rows_stored[par], 16)

            def expert_round(r):
                if r:
                    act.wait_ge(rows_added, TT * TOPK * r)
                with act.Fori(0, E // 4) as i:
                    for q in range(4):
                        expert(r, i, q)
                for par in range(2):
                    act.wait_ge(rows_stored[par], 16 * ((E // 2) * (r + 1) + 1))
                act.sem_inc(all_written, 1)
            for par in range(2):
                act.sem_inc(rows_stored[par], 16)
            act.sem_inc(down_free, 2)
            rounds(act, expert_round)
            for j in range(TT):
                act.wait_ge(lnv_ready, TT + j + 1)
                link(fn(rst[:, j:j + 1], rt[:, 0, 2 * j + 1:2 * j + 2], ACT.Ln, bias=eps))
                fn(rst[:, j:j + 1], rst[:, j:j + 1], ACT.Exp, scale=-0.5).then_inc(rstd1_ready, 1)

        @block.vector
        def _(dve):
            V = nc.vector
            steps = {dve_step: 0, overflow_step: 0}
            now = [dve_step]

            def link(ins):
                steps[now[0]] += 1
                ins.then_inc(now[0], 1)
                dve.wait_ge(now[0], steps[now[0]])

            dve.wait_ge(cst_loaded, 16)

            def rope(out, src, cos, sin, t):
                a1, a2 = src[..., 0:16], src[..., 16:32]
                link(V.tensor_tensor(t[0], a1, cos, ALU.mult))
                link(V.tensor_tensor(t[1], a2, sin, ALU.mult))
                link(V.tensor_tensor(out[..., 0:16], t[0], t[1], ALU.subtract))
                link(V.tensor_tensor(t[0], a1, sin, ALU.mult))
                link(V.tensor_tensor(t[1], a2, cos, ALU.mult))
                link(V.tensor_tensor(out[..., 16:32], t[0], t[1], ALU.add))

            def prep(n):
                kind, g, i, q, rows, keys = U[n]
                if n == 0:
                    link(V.memset(qbd_fox, 0.0))
                    link(V.memset(qbd_mem, 0.0))
                if n >= 1 and kind == "fox":
                    dve.wait_ge(done["S"], n)
                if kind == "fox" and (g == "s" or q == 0):
                    dve.wait_ge(free["V"], done_at("V", "c", i if g == "s" else "p"))
                if kind == "fox" and g == "p" and q == 0:
                    link(V.tensor_scalar(LH, FX, cc("oh")[:, i:i + 1], None, ALU.mult))
                if g == "s" and kind == "mla":
                    if i == 0:
                        dve.wait_ge(logf_loaded, 16)
                        link(V.memset(LFc[0], 0.0))
                        link(V.memset(LFc[1], 0.0))
                    link(V.tensor_scalar(LFc[i % 2][:, :, 0:8], lfc_raw[:, 2 * i:2 * i + 2, :], -1.0, None, ALU.mult))
                    link(V.tensor_copy(LFc[i % 2][:, :, 32:40], lfc_raw[:, 2 * i:2 * i + 2, :]))
                if g == "s" and kind == "fox":
                    ts = slice(256 + NQ * i, 256 + NQ * (i + 1))
                    fx = FX[:, 0:NQ].unsqueeze(1).to_broadcast([P, H, NQ])
                    oh = cc("oh").unsqueeze(2).to_broadcast([P, H, NQ])
                    link(V.tensor_tensor(LH[:, 0:P].rearrange("p (h q) -> p h q", h=H), fx, oh, ALU.mult))
                    v = qbd_fox.rearrange("p (m c) -> p m c", c=160)
                    for half in range(2):
                        r = slice(half * 64, half * 64 + 64)
                        link(V.tensor_copy(v[r, :, half * NQ:(half + 1) * NQ], fqT[r, :, ts]))
                if g == "s" and kind == "mem":
                    ts = slice(256 + NQ * i, 256 + NQ * (i + 1))
                    dve.wait_ge(done["S"], n)
                    v = qbd_mem.rearrange("p (m c) -> p m c", c=80)
                    link(V.tensor_copy(v[:, :, 0:NQ], mqT[:, :, ts]))
                dve.sem_inc(prep_ready, 1)

            def layer_norm(base, ready):
                for j in range(TT):
                    st6 = rt[:, 1, 16 * j:16 * j + 12]
                    link(V.bn_stats(st6[:, 0:6], x_sb[:, j, 0:512]))
                    link(V.bn_stats(st6[:, 6:12], x_sb[:, j, 512:D]))
                    V.bn_aggr(rt[:, 0, 2 * j:2 * j + 2], st6).then_inc(lnv_ready, 1)
                for j in range(TT):
                    dve.wait_ge(rstd1_ready, base + j + 1)
                    xv = x_sb[:, j, :]
                    link(V.tensor_scalar(xv, xv, rt[:, 0, 2 * j:2 * j + 1], rst[:, j:j + 1], ALU.subtract, ALU.mult))
                    link(V.tensor_tensor(xv, xv, lngb[:, 0:D], ALU.mult))
                    V.tensor_tensor(xv, xv, lngb[:, D:2 * D], ALU.add).then_inc(ready, 1)

            def route():
                link(V.memset(TGP, 0.0))
                dve.wait_ge(ez_ready, 1)
                link(V.tensor_scalar(sel, sel, 1.0, None, ALU.add))
                link(V.reciprocal(sc, sel))
                link(V.tensor_tensor(sel, sc, rb_b.unsqueeze(1).to_broadcast([P, TT, E]), ALU.add))
                for j in range(TT):
                    for g in range(NG):
                        ins = V.max(g8[:, j * NG + g, :], sel[:, j, g * 8:(g + 1) * 8])
                link(ins)
                link(V.tensor_tensor(gs, g8[:, :, 0], g8[:, :, 1], ALU.add))
                for j in range(TT):
                    gk = gs[:, j * 8:(j + 1) * 8].unsqueeze(1).to_broadcast([P, 8, 8])
                    gi = gs[:, j * 8:(j + 1) * 8].unsqueeze(2).to_broadcast([P, 8, 8])
                    t1 = masked[:, j, :].rearrange("p (i k) -> p i k", i=8)
                    t2 = rep[:, j, :].rearrange("p (i k) -> p i k", i=8)
                    link(V.tensor_tensor(t1, gk, gi, ALU.is_gt))
                    link(V.tensor_tensor(t2, gk, gi, ALU.is_equal))
                    link(V.tensor_tensor(rep[:, j, :], rep[:, j, :], cc("before"), ALU.mult))
                    link(V.tensor_tensor(t1, t1, t2, ALU.add))
                    link(V.tensor_reduce(gm[:, j * 8:(j + 1) * 8], t1, AX, ALU.add))
                link(V.tensor_scalar(gm, gm, float(TG), None, ALU.is_lt))
                for j in range(TT):
                    mb = gm[:, j * 8:(j + 1) * 8].unsqueeze(2).to_broadcast([P, 8, 8])
                    sv = sel[:, j, :].rearrange("p (g c) -> p g c", g=8)
                    mv = masked[:, j, :].rearrange("p (g c) -> p g c", g=8)
                    link(V.tensor_tensor(mv, sv, mb, ALU.mult))
                link(V.tensor_scalar(gm, gm, 1.0, 1e30, ALU.subtract, ALU.mult))
                for j in range(TT):
                    mb = gm[:, j * 8:(j + 1) * 8].unsqueeze(2).to_broadcast([P, 8, 8])
                    mv = masked[:, j, :].rearrange("p (g c) -> p g c", g=8)
                    link(V.tensor_tensor(mv, mv, mb, ALU.add))
                    link(V.max(t8[:, j, :], masked[:, j, :]))
                    link(V.match_replace(rep[:, j, :], t8[:, j, :], masked[:, j, :], -3e38))
                V.tensor_tensor(mask, rep, masked, ALU.not_equal).then_inc(mask_ready, 1)
                dve.wait_ge(mask_ready, 1)
                link(V.tensor_tensor(rep, sc, mask, ALU.mult))
                link(V.tensor_reduce(wsum, rep, AX, ALU.add))
                link(V.reciprocal(wsum, wsum))
                for j in range(TT):
                    link(V.tensor_scalar(tgp4[:, j, 0:E, 1], rep[:, j, :], wsum[:, j:j + 1], 2.5, ALU.mult, ALU.mult))
                    link(V.tensor_scalar(tgp4[:, j, 0:E, 0], mask[:, j, :], 0.0, cc("tok")[:, j:j + 1], ALU.mult, ALU.add))

            def tables():
                dve.wait_ge(free["V"], done_at("V", "pos", TT - 1))
                link(V.scalar_tensor_tensor(rep, tmp3, 1.0, mask, ALU.add, ALU.mult))
                V.tensor_reduce(cmax, rep, mybir.AxisListType.XY, ALU.max).then_inc(count_ready, 1)
                link(V.memset(tgp4[:, :, :, 2], -1.0))
                link(V.tensor_scalar(tgp4[:, :, 0:E, 2], rep, -1.0, None, ALU.add))
                rows_of_round()

            def rows_of_round():
                at = tgp4[:, :, 0:E, 2]
                link(V.tensor_scalar(rep, at, 0.0, None, ALU.is_ge))
                link(V.tensor_scalar(tmp3, at, float(CAP), None, ALU.is_lt))
                link(V.tensor_tensor(rep, rep, tmp3, ALU.mult))
                link(V.tensor_tensor(slot_row, at, cc("slot0").unsqueeze(1).to_broadcast([P, TT, E]), ALU.add))
                link(V.scalar_tensor_tensor(slot_row, slot_row, 1.0, rep, ALU.add, ALU.mult))
                for j in range(TT):
                    link(V.max(t8[:, j, :], slot_row[:, j, :]))
                t24 = t8.rearrange("p j k -> p (j k)")
                link(V.tensor_scalar(gs, t24, 0.0, float(E * CAP + 1), ALU.is_equal, ALU.mult))
                V.scalar_tensor_tensor(row_idx[:, :], t24, -1.0, gs, ALU.add, ALU.add).then_inc(row_idx_ready, 1)

            for st in PLAN:
                ring, key = st[0], st[1:]
                if ring == "T":
                    dve.wait_ge(done["T"], done_at(*st))
                    src = ps["T"][pos_in[st] % 2]
                    src4 = src[:, :].rearrange("p (k t) -> p k t", k=4)
                    if key[0] in ("x", "mem", "y", "x1"):
                        dst = {"x": xT, "mem": memT, "y": yT, "x1": xT}[key[0]]
                        _, j, half = key
                        last = V.tensor_copy(dst[:, half * 4:half * 4 + 4, j * P:(j + 1) * P], src4)
                    elif key[0] == "uk":
                        last = V.tensor_copy(wukT[0:64, key[1] * 4:key[1] * 4 + 4, :], src4[0:64])
                    elif key[0] == "lat":
                        ts = slice(key[1] * P, (key[1] + 1) * P)
                        V.tensor_copy(qnT[:, :, ts], src4[:, 0:2, :])
                        V.tensor_copy(latT[:, ts], src4[:, 2, :])
                        last = V.tensor_copy(krT[0:RD, ts], src4[0:RD, 3, :])
                    elif key[0] == "qr":
                        _, j, half = key
                        if j < 2:
                            last = V.tensor_copy(qrP[0:RD, half * 4:half * 4 + 4, j * P:(j + 1) * P], src4[0:RD])
                        else:
                            last = V.tensor_copy(
                                qrS[0:RD].rearrange("p b (h q) -> p h b q", h=H)[:, half * 4:half * 4 + 4],
                                src[0:RD, :].rearrange("p (h b q) -> p h b q", h=4, b=NB))
                    elif key[0] == "fk":
                        last = V.tensor_copy(fkT[:, :, key[1] * P:(key[1] + 1) * P], src4)
                    elif key[0] == "mk":
                        last = V.tensor_copy(mkT[:, :, key[1] * P:(key[1] + 1) * P], src4)
                    elif key[0] == "clat":
                        b = key[1]
                        n = next(i for i, u in enumerate(U) if u[:3] == ("mla", "s", b))
                        dve.wait_ge(done["S"], n - 2)
                        V.tensor_copy(latTc.rearrange("p (t c) -> p t c", t=2), src4[:, 0:2, :])
                        last = V.tensor_copy(krTc[0:RD].rearrange("p (t c) -> p t c", t=2), src4[0:RD, 2:4, :])
                    elif key[0] in ("cfk", "cmk"):
                        _, b, t = key
                        kd = "fox" if key[0] == "cfk" else "mem"
                        n = next(i for i, u in enumerate(U) if u[:3] == (kd, "s", b))
                        dve.wait_ge(done["S"], n - 2)
                        dst = fkTc if key[0] == "cfk" else mkTc
                        last = V.tensor_copy(dst[:, :, t * P:(t + 1) * P], src4)
                    elif key[0] == "p":
                        n = key[1]
                        rows, nk = unit_stage(n)
                        if n >= 2:
                            dve.wait_ge(done["V"], done_at("V", "o", n - 2))
                        if rows == P:
                            last = V.tensor_copy(pT[n % 2][:, 0:nk * P], src[:, 0:nk * P])
                        else:
                            last = V.tensor_copy(pT[n % 2].rearrange("p (t r) -> p t r", t=3)[:, 0:nk, 0:rows],
                                                 src4[:, 0:nk, 0:rows])
                    last.then_inc(free["T"], 1)
                elif ring == "rms":
                    dve.wait_ge(free["P"], done_at("P", "lat", 2))
                    dve.wait_ge(vec_loaded, 48)
                    for j in range(TT):
                        link(V.tensor_tensor_reduce(scr, lat_raw[:, j, 0:QL], lat_raw[:, j, 0:QL], 1.0, 0.0,
                                                    ALU.mult, ALU.add, ssq[:, j:j + 1]))
                        ins = V.tensor_tensor_reduce(scr[:, 0:KVL], lat_raw[:, j, QL:QL + KVL], lat_raw[:, j, QL:QL + KVL],
                                                     1.0, 0.0, ALU.mult, ALU.add, ssq[:, 3 + j:4 + j])
                        if j < TT - 1:
                            link(ins)
                    ins.then_inc(sq_ready, 1)
                    z = lft[:, 0, :].rearrange("p (j h) -> p j h", j=TT)
                    link(V.tensor_tensor(z, lat_raw[:, :, 416:424], b_f_b.unsqueeze(1).to_broadcast([P, TT, 8]), ALU.add))
                    link(V.tensor_scalar(lft[:, 1, :], lft[:, 0, :], -1.0, None, ALU.mult))
                    V.tensor_tensor(lft[:, 1, :], lft[:, 0, :], lft[:, 1, :], ALU.min).then_inc(nz_ready, 1)
                    cosk, sink = rope_t[:, :, 0:16], rope_t[:, :, 16:32]
                    tmp = [rt[:, i, 0:48].rearrange("p (j c) -> p j c", j=TT) for i in range(2)]
                    rope(kr_rot, lat_raw[:, :, 384:416], cosk, sink, tmp)
                    dve.wait_ge(rstd_ready, 1)
                    for j in range(TT):
                        V.scalar_tensor_tensor(qn[:, j, :], lat_raw[:, j, 0:QL], rst[:, j:j + 1], gq_b, ALU.mult, ALU.mult)
                        ins = V.scalar_tensor_tensor(latn[:, j, :], lat_raw[:, j, QL:QL + KVL], rst[:, 3 + j:4 + j], gkv_b,
                                                     ALU.mult, ALU.mult)
                    ins.then_inc(lat_ready, 1)
                    link(V.memset(LFn, 0.0))
                    dve.wait_ge(lse_ready, 1)
                    link(V.tensor_scalar(lft[:, 0, :], lft[:, 0, :], 0.0, None, ALU.min))
                    lf_flat = lf_new.rearrange("p j h -> p (j h)")
                    link(V.tensor_tensor(lf_flat, lft[:, 0, :], lft[:, 3, :], ALU.subtract))
                    V.tensor_scalar(LFn[:, :, 0:8], lf_new, -1.0, None, ALU.mult)
                    V.tensor_copy(LFn[:, :, 32:40], lf_new).then_inc(logf_ready, 1)
                elif ring == "qrope":
                    j = key[0]
                    dve.wait_ge(free["P"], done_at("P", "qr", j))
                    c = rope_t[:, j, 0:16].unsqueeze(1).to_broadcast([P, H, 16])
                    s = rope_t[:, j, 16:32].unsqueeze(1).to_broadcast([P, H, 16])
                    tmp = [rt[:, i, 0:128].rearrange("p (h c) -> p h c", h=H) for i in range(2)]
                    rope(qr_rot[:, j, :].rearrange("p (h c) -> p h c", h=H), qr_tok[:, j, :].rearrange("p (h c) -> p h c", h=H),
                         c, s, tmp)
                    dve.sem_inc(qrope_ready, 1)
                elif ring == "prep":
                    prep(key[0])
                elif ring == "S":
                    n = key[0]
                    rows, nk = unit_stage(n)
                    dve.wait_ge(done["S"], n + 1)
                    V.tensor_reduce(mx[0:rows, n:n + 1], ps["S"][n % 2][0:rows, 0:nk * P], AX, ALU.max, negate=True)\
                        .then_inc(max_ready, 1)
                elif ring == "norm":
                    n = key[0]
                    rows, nk = unit_stage(n)
                    dve.wait_ge(exp_ready, n + 1)
                    dve.sem_inc(free["S"], 1)
                    link(V.reciprocal(rs[0:rows, n:n + 1], sm[0:rows, n:n + 1]))
                    pv = prob[n % 3][0:rows, 0:nk * P]
                    V.tensor_scalar(pv, pv, rs[0:rows, n:n + 1], None, ALU.mult).then_inc(norm_ready, 1)
                elif ring == "V":
                    dve.wait_ge(done["V"], done_at(*st))
                    src = ps["V"][pos_in[st] % 2]
                    if key[0] == "c":
                        w = 256 if key[1] == "p" else T
                        if key[1] == "p":
                            link(V.memset(FX, 1.0))
                            link(V.memset(FR, 0.0))
                            V.memset(FR[32:40, :], 1.0)
                            V.tensor_copy(FX[32:40, :], src[32:40, 0:256])
                        else:
                            n = next(i for i, u in enumerate(U) if u[:3] == ("fox", "s", key[1]))
                            dve.wait_ge(done["S"], n - 2)
                            q0 = 256 + NQ * key[1]
                            V.tensor_copy(FX[32:40, 0:NQ], src[32:40, q0:q0 + NQ])
                        last = V.tensor_copy(FR[0:32, 0:w], src[0:32, 0:w])
                    elif key[0] == "o":
                        kind, g, i, q, rows, keys = U[key[1]]
                        if kind == "mla":
                            if key[1] >= 2 and U[key[1] - 2][0] == "mla":
                                dve.wait_ge(done["V"], done_at("V", "ov", key[1] - 2))
                            elif g == "s" and i > 0:
                                dve.wait_ge(done["V"], done_at("V", "ov", key[1] - 3))
                            last = V.tensor_copy(olat[key[1] % 2], src[:, 0:P])
                        elif g == "p":
                            br = 1 if kind == "fox" else 2
                            h0, hn, blkk = ((i % 2) * 64, 64, i // 2) if kind == "fox" else (0, P, i)
                            last = V.tensor_copy(oT[h0:h0 + hn, br, blkk, q * P:(q + 1) * P], src[h0:h0 + hn, 0:P])
                        elif kind == "fox":
                            sv = src[:, 0:P].rearrange("p (m c) -> p m c", m=4)
                            ts = slice(256 + NQ * i, 256 + NQ * (i + 1))
                            V.tensor_copy(oT[0:64, 1, :, ts], sv[0:64, :, 0:NQ])
                            last = V.tensor_copy(oT[64:P, 1, :, ts], sv[64:P, :, NQ:2 * NQ])
                        else:
                            ts = slice(256 + NQ * i, 256 + NQ * (i + 1))
                            last = V.tensor_copy(oT[:, 2, :, ts], src[:, 0:64].rearrange("p (m c) -> p m c", m=4))
                    elif key[0] == "ov":
                        kind, g, i, q, rows, keys = U[key[1]]
                        if g == "p":
                            h0 = (i % 2) * 64
                            last = V.tensor_copy(oT[h0:h0 + 64, 0, i // 2, q * P:(q + 1) * P], src[h0:h0 + 64, 0:P])
                        else:
                            ts = slice(256 + NQ * i, 256 + NQ * (i + 1))
                            last = V.tensor_copy(oT[:, 0, :, ts], src[:, 0:64].rearrange("p (m c) -> p m c", m=4))
                    elif key[0] == "b":
                        _, br, cb, j = key
                        dve.wait_ge(free["P"], done_at("P", "g", br, cb, j))
                        n = (br * 2 + cb) * TT + j
                        e = egate[n % 2]
                        link(V.tensor_scalar(e, e, 1.0, None, ALU.add))
                        link(V.reciprocal(e, e))
                        yv = y[:, j, cb * 512:(cb + 1) * 512]
                        if br:
                            dve.wait_ge(free["V"], done_at("V", "b", br - 1, cb, j))
                        if br == 0:
                            last = V.tensor_tensor(yv, src[:, :], e, ALU.mult)
                        else:
                            link(V.tensor_tensor(e, src[:, :], e, ALU.mult))
                            last = V.tensor_tensor(yv, yv, e, ALU.add)
                    elif key[0] == "out":
                        _, j, half = key
                        cs = slice(half * 512, (half + 1) * 512)
                        last = V.scalar_tensor_tensor(x_sb[:, j, cs], x_sb[:, j, cs], ALPHA, src[:, :], ALU.mult, ALU.add)
                    elif key[0] == "router":
                        last = V.tensor_copy(sc[:, key[1], :], src[:, 0:E])
                    elif key[0] == "pos":
                        last = V.tensor_copy(tmp3[:, key[1], :], src[:, 0:E])
                    elif key[0] == "flag":
                        link(V.tensor_reduce(wsum[0:1, 0:1], src[0:1, 0:P], AX, ALU.max))
                        V.tensor_copy(flag_i[0:1, 0:1], wsum[0:1, 0:1]).then_inc(flag_ready, 1)
                        last = V.tensor_copy(wsum[0:1, 1:2], wsum[0:1, 0:1])
                    elif key[0] == "shd":
                        _, j, half = key
                        dve.wait_ge(x1_stored, 16)
                        cs = slice(half * 512, (half + 1) * 512)
                        last = V.scalar_tensor_tensor(x_sb[:, j, cs], x_sb[:, j, cs], ALPHA, src[:, :], ALU.mult, ALU.add)
                    last.then_inc(free["V"], 1)
                    if key == ("router", 2):
                        dve.wait_ge(free["V"], done_at(*st))
                        dve.sem_inc(z_ready, 1)
                elif ring == "ln1":
                    dve.wait_ge(free["V"], done_at("V", "out", 2, 1))
                    dve.wait_ge(ln_loaded, 32)
                    layer_norm(0, x1_ready)
                elif ring == "route":
                    route()
                elif ring == "tables":
                    tables()
                elif ring == "shact":
                    dve.wait_ge(free["P"], done_at("P", "sh", 3))
                    V.tensor_tensor(sh_sil, sh_sil, sh_up, ALU.mult).then_inc(hidden_ready, 1)

            def build_onehot(r, e, par):
                V.tensor_copy(pcol[par], tgp4[:, :, bass.ds(e, 1), :].rearrange("p j o c -> p j (o c)")).then_inc(column_copied, 1)
                dve.wait_ge(column_copied, (E + 3) * r + e + 1)
                for j in range(TT):
                    ins = V.tensor_scalar(onehot[par][:, j, :], cc("iota"), pcol[par][:, j, 2:3], None, ALU.is_equal)
                ins.then_inc(onehot_built, 1)

            def copy_slots(r, e, par, g):
                dve.wait_ge(slots_done, (E + 2) * r + e + 1)
                V.tensor_copy(gslot[0:CAP, g:g + 1], ps["S"][par][0:CAP, 1:2])
                V.tensor_copy(idx[0:CAP, par:par + 1], ps["S"][par][0:CAP, 0:1]).then_inc(idx_ready, 1)

            def take_turned(r, e, par):
                dve.wait_ge(xg_turned, 2 * ((E + 1) * r + e) + 1)
                V.tensor_copy(xgT[par][:, 0:4, :], ps["T"][0][:, 0:4 * CAP].rearrange("p (k c) -> p k c", k=4)).then_inc(xgT_ready, 1)
                dve.wait_ge(xg_turned, 2 * ((E + 1) * r + e) + 2)
                V.tensor_copy(xgT[par][:, 4:8, :], ps["T"][1][:, 0:4 * CAP].rearrange("p (k c) -> p k c", k=4)).then_inc(xgT_ready, 1)

            def expert(r, i, q):
                e, par = i * 4 + q, q % 2
                copy_slots(r, e + 2, par, (q + 2) % 4)
                take_turned(r, e + 1, 1 - par)
                dve.wait_ge(silu_ready, E * r + e + 1)
                V.tensor_tensor(hid[par], sil[par], ps["P"][par][:, 2 * CAP:4 * CAP].rearrange("p (m c) -> p m c", m=2), ALU.mult)\
                    .then_inc(hid_ready, 1)
                build_onehot(r, e + 3, 1 - par)

            def expert_round(r):
                if r:
                    now[0] = overflow_step
                    link(V.tensor_scalar(tgp4[:, :, :, 2], tgp4[:, :, :, 2], -float(CAP), None, ALU.add))
                    rows_of_round()
                build_onehot(r, 0, 0)
                build_onehot(r, 1, 1)
                copy_slots(r, 0, 0, 0)
                build_onehot(r, 2, 0)
                copy_slots(r, 1, 1, 1)
                take_turned(r, 0, 0)
                with dve.Fori(0, E // 4) as i:
                    for q in range(4):
                        expert(r, i, q)
                for n in range(TT * TOPK):
                    j = n // TOPK
                    dve.wait_ge(rows_gathered[n], 16 * (r + 1))
                    V.tensor_tensor(x_sb[:, j, :], x_sb[:, j, :], gathered_rows[:, n, :], ALU.add).then_inc(rows_added, 1)
                    dve.wait_ge(rows_added, TT * TOPK * r + n + 1)
                now[0] = dve_step
            dve.sem_inc(hid_ready, 2)
            rounds(dve, expert_round)
            dve.wait_ge(ln2_loaded, 32)
            layer_norm(TT, out_ready)



_INS = ["x_prompt", "x_sample", "mem_prompt", "cache_mla_latent", "cache_mla_krope", "cache_fox_k", "cache_fox_v",
        "cache_fox_logf", "cache_mem_k", "cache_mem_v", "ln1_g", "ln1_b", "w_in", "b_f", "q_norm_g", "w_q_up",
        "kv_norm_g", "w_kv_up", "w_mem_k", "w_mem_v", "w_br_mla", "w_br_fox", "w_br_mem", "w_out", "ln2_g", "ln2_b",
        "w_router", "router_bias", "w_e_gate", "w_e_up", "w_e_down", "w_s_gate", "w_s_up", "w_s_down"]
_OUTS = [("y_prompt", (1, 256, 1024)), ("y_sample", (8, 16, 1024)), ("p_mla_latent", (1, 1, 256, 128)),
         ("p_mla_krope", (1, 1, 256, 32)), ("p_fox_k", (1, 1, 256, 8, 64)), ("p_fox_v", (1, 1, 256, 8, 64)),
         ("p_fox_logf", (1, 1, 256, 8)), ("p_mem_k", (1, 1, 256, 4, 128)), ("p_mem_v", (1, 1, 256, 4, 128)),
         ("s_mla_latent", (1, 8, 16, 128)), ("s_mla_krope", (1, 8, 16, 32)), ("s_fox_k", (1, 8, 16, 8, 64)),
         ("s_fox_v", (1, 8, 16, 8, 64)), ("s_fox_logf", (1, 8, 16, 8))]


def kernel(**inputs):
    import concourse.bacc as bacc
    from concourse.bass_utils import run_bass_kernel_spmd

    nc = bacc.Bacc("TRN2", target_bir_lowering=False, num_devices=1)
    arrays, a = {}, {}
    for name in _INS:
        v = np.ascontiguousarray(inputs[name])
        arrays[name] = v
        a[name] = nc.dram_tensor(name, v.shape, F32, kind="ExternalInput").ap()
    arrays["consts"] = constants()
    a["consts"] = nc.dram_tensor("consts", (P, NCST), F32, kind="ExternalInput").ap()
    outs = {n: nc.dram_tensor(n, s, F32, kind="ExternalOutput").ap() for n, s in _OUTS}
    arrays["zero_row"] = np.zeros((1, D), np.float32)
    a["zero_row"] = nc.dram_tensor("zero_row", (1, D), F32, kind="ExternalInput").ap()
    build(nc, a, outs)
    r = run_bass_kernel_spmd(nc, [arrays], core_ids=[0])
    return tuple(r.results[0][n] for n, _ in _OUTS)
```

```python
from contextlib import ExitStack

import numpy as np

import concourse.bass as bass
from concourse import mybir

F32 = mybir.dt.float32
I32 = mybir.dt.int32
ALU = mybir.AluOpType
ACT = mybir.ActivationFunctionType
AX = mybir.AxisListType.X

P = 128
D = 1024
KD = D // P
SEQ, NB, NQ, PAST, NMEM = 256, 8, 16, 256, 256
TT = 3
T = TT * P
H, HM = 8, 4
QL, KVL, RD, ND = 256, 128, 32, 64
CHUNK = 64
E, TOPK, NG, TG = 64, 8, 8, 4
FE = 256
CAP = 3 * T * TOPK // (2 * E)
ROUNDS = -(-T // CAP)
AHEAD = 3
GATHERS = [(E + AHEAD - q + 3) // 4 for q in range(4)]
ALPHA = 2.0 ** 0.25
EPS = 1e-5
NEG = -1e30
MLA_SCALE = float(96 ** -0.5)
FOX_SCALE = 0.125
MEM_SCALE = float(128 ** -0.5)
OFF = {}
_o = 0
for _n, _w in (("qlat", 256), ("ckv", 128), ("kr", 32), ("fq", 512), ("fk", 512), ("fv", 512), ("fl", 8), ("mq", 512), ("g", 3072)):
    OFF[_n] = _o
    _o += _w

CST = {}
_c = 0
for _n, _w in (("ident", 128), ("tri", 128), ("ones", 256), ("blk", 128), ("strict", 128), ("causal", 128),
               ("chunk", 128), ("wfox", 240), ("wmla", 240), ("rope", 96), ("iota", CAP), ("tok", 3),
               ("oh", 8), ("eps", 1), ("unused", 1), ("before", 64)):
    CST[_n] = (_c, _w)
    _c += _w
NCST = _c


def constants():
    c = np.zeros((P, NCST), np.float32)

    def put(name, a):
        o, w = CST[name]
        c[:a.shape[0], o:o + w] = a
    s = np.arange(P)[:, None]
    t = np.arange(P)[None, :]
    put("ident", np.eye(P))
    put("tri", s <= t)
    put("ones", np.ones((P, 256)))
    put("blk", (s // NQ == t // NQ) & (s <= t))
    put("strict", s < t)
    put("causal", np.where(t <= s, 0.0, NEG))
    put("chunk", np.where(t // CHUNK <= s // CHUNK, 0.0, NEG))
    w = np.arange(240)[None, :] - 7 * NQ
    own = (w >= 0) & (w < NQ)
    put("wfox", np.where(own & (w <= s % NQ), 0.0, NEG))
    put("wmla", np.where(own & (s >= 0), 0.0, NEG))
    half = RD // 2
    inv = np.float32(10000.0) ** (-np.arange(half, dtype=np.float32) / np.float32(half))
    pos = np.concatenate([np.arange(SEQ), PAST + np.arange(P) % NQ]).astype(np.float32)
    ang = (pos[:, None] * inv[None, :]).astype(np.float32)
    cs = np.concatenate([np.cos(ang), np.sin(ang)], 1).reshape(TT, P, RD).transpose(1, 0, 2)
    put("rope", cs.reshape(P, TT * RD))
    put("iota", np.broadcast_to(np.arange(CAP), (P, CAP)))
    put("tok", s + P * np.arange(TT)[None, :])
    oh = np.zeros((40, 8))
    oh[0:8] = np.eye(8)
    oh[32:40] = np.eye(8)
    put("oh", oh)
    put("eps", np.full((P, 1), EPS))
    put("unused", 4096 + s)
    put("before", np.broadcast_to((np.arange(8)[None, :] < np.arange(8)[:, None]).reshape(1, 64), (P, 64)))
    return c


def units():
    u = []
    for h in range(H):
        for q in range(2):
            u.append(("mla", "p", h, q, P, (q + 1) * P))
    for h in range(H):
        for q in range(2):
            u.append(("fox", "p", h, q, P, (q + 1) * P))
    for h in range(HM):
        for q in range(2):
            u.append(("mem", "p", h, q, P, NMEM))
    for b in range(NB):
        u += [("mla", "s", b, 0, P, 3 * P), ("fox", "s", b, 0, P, 3 * P), ("mem", "s", b, 0, 64, NMEM)]
    return u


def w_units():
    w = []

    def both(name, col, n):
        w.append((name, 0, col, n))
        w.append((name, 4, col, n))
    both("lat", 0, 416)
    both("in", OFF["fk"], 512)
    both("in", OFF["fv"], 512)
    both("in", OFF["fq"], 512)
    both("in", OFF["mq"], 512)
    both("mem_k", 0, 512)
    both("mem_v", 0, 512)
    for c in range(6):
        both("in", OFF["g"] + c * 512, 512)
    for br in ("br_mla", "br_fox", "br_mem"):
        w += [(br, 0, 0, 512), (br, 0, 512, 512)]
    both("out", 0, 512)
    both("out", 512, 512)
    w += [("s_gate",), ("s_up",), ("s_down",)]
    return w


def plan():
    U = units()
    s = []
    for j in range(TT):
        for half in range(2):
            s.append(("T", "x", j, half))
    for j in range(TT):
        s.append(("P", "lat", j))
    s.append(("rms",))
    for j in range(2):
        for half in range(2):
            s.append(("T", "mem", j, half))
    s += [("T", "uk", 0), ("T", "uk", 1)]
    s += [("P", "fk", j) for j in range(TT)]
    s += [("P", "fv", j) for j in range(TT)]
    s += [("T", "lat", j) for j in range(TT)]
    for j in range(TT):
        s.append(("P", "qr", j))
        s.append(("qrope", j))
        s.append(("T", "fk", j))
        s.append(("T", "qr", j, 0))
        s.append(("T", "qr", j, 1))
    s += [("P", "fq", m) for m in range(4)]
    for h in range(H):
        s.append(("P", "qn", h))
        if h:
            s.append(("P", "qa", h - 1))
    s.append(("P", "qa", H - 1))
    s += [("P", "mq", m) for m in range(4)]
    s += [("P", "mk", j) for j in range(2)]
    s += [("P", "mv", j) for j in range(2)]
    s += [("T", "mk", j) for j in range(2)]
    s.append(("V", "c", "p"))

    def load_keys(n):
        k, g, b = U[n][:3]
        if g != "s":
            return
        if k == "mla":
            s.append(("T", "clat", b))
        elif k == "fox":
            s.append(("T", "cfk", b, 0))
            s.append(("T", "cfk", b, 1))
            s.append(("V", "c", b))
        else:
            s.append(("T", "cmk", b, 0))
            s.append(("T", "cmk", b, 1))
    pieces = [(n, k) for n in range(6 * TT) for k in range(0, KD, 2)]

    def gate_piece():
        n, k = pieces.pop(0)
        s.append(("P", "g", n) if k == KD - 2 else ("gpiece", n, k))
    n_u = len(U)
    for n in range(n_u + 4):
        if n < n_u:
            if n == 0:
                s.append(("prep", 0))
            s.append(("S", n))
            if n + 1 < n_u:
                load_keys(n + 1)
                s.append(("prep", n + 1))
            gate_piece()
            if n % 8 == 7:
                gate_piece()
        if 1 <= n <= n_u:
            s.append(("norm", n - 1))
        if 2 <= n <= n_u + 1:
            s.append(("T", "p", n - 2))
        if 3 <= n <= n_u + 2:
            s.append(("V", "o", n - 3))
        if n >= 4 and U[n - 4][0] == "mla":
            s.append(("V", "ov", n - 4))
    while pieces:
        gate_piece()
    for br in range(3):
        for cb in range(2):
            for j in range(TT):
                s.append(("V", "b", br, cb, j))
    for j in range(TT):
        for half in range(2):
            s.append(("T", "y", j, half))
    for half in range(2):
        for j in range(TT):
            s.append(("V", "out", j, half))
    s.append(("ln1",))
    for j in range(TT):
        for half in range(2):
            s.append(("T", "x1", j, half))
    for j in range(TT):
        s.append(("V", "router", j))
    for m in range(4):
        s.append(("P", "sh", m))
    s.append(("route",))
    for j in range(TT):
        s.append(("V", "pos", j))
    s.append(("tables",))
    s.append(("V", "flag"))
    s.append(("shact",))
    for j in range(TT):
        for half in range(2):
            s.append(("V", "shd", j, half))
    return s


def build(nc, a, outs):
    U = units()
    PLAN = plan()
    WU = w_units()
    NW = 4
    pos_in = {}
    count = {"P": 0, "S": 0, "T": 0, "V": 0}
    for st in PLAN:
        if st[0] in count:
            pos_in[st] = count[st[0]]
            count[st[0]] += 1

    def done_at(*st):
        return pos_in[st] + 1

    last_use = []
    names = ["lat", "fk", "fv", "fq", "mq", "mk", "mv"]
    for nme in names:
        lu = {"lat": ("P", "lat", 2), "fk": ("P", "fk", 2), "fv": ("P", "fv", 2), "fq": ("P", "fq", 3),
              "mq": ("P", "mq", 3), "mk": ("P", "mk", 1), "mv": ("P", "mv", 1)}[nme]
        last_use += [lu, lu]
    for c in range(6):
        last_use += [("P", "g", 3 * c + 2)] * 2
    for br in range(3):
        for cb in range(2):
            last_use.append(("V", "b", br, cb, 2))
    last_use += [("V", "out", 2, 0), ("V", "out", 2, 0), ("V", "out", 2, 1), ("V", "out", 2, 1)]
    last_use += [("P", "sh", 1), ("P", "sh", 3), ("V", "shd", 2, 1)]
    assert len(last_use) == len(WU)
    PROJ_STORES = 12
    first_of = {"lat": 0, "fk": 2, "fv": 4, "fq": 6, "mq": 8, "mk": 10, "mv": 12, "g": 14, "br": 26, "out": 32, "s_gate": 36, "s_up": 37, "s_down": 38}

    with ExitStack() as ctx:
        def region(name, cols):
            return ctx.enter_context(nc.sbuf_tensor(name, [P, cols], F32))

        def sem(name):
            return ctx.enter_context(nc.semaphore(name))

        class Space:

            def __init__(self, reg, cols, at=0):
                self.reg, self.cols, self.at = reg, cols, at

            def take(self, *shape):
                n = int(np.prod(shape))
                v = self.reg[:, self.at:self.at + n]
                self.at += n
                assert self.at <= self.cols, (self.at, self.cols)
                if len(shape) == 2:
                    v = v.rearrange("p (a b) -> p a b", b=shape[1])
                if len(shape) == 3:
                    v = v.rearrange("p (a b c) -> p a b c", b=shape[1], c=shape[2])
                return v

        cst = region("cst", NCST)
        lngb_cols, o_cols, y_cols, w_cols, a_cols, m_cols = 2048, 4608, 3072, NW * 2048, 24576, 2660
        lngb = region("lngb", lngb_cols)
        x_sb = region("x_sb", 3072)[:, :].rearrange("p (j d) -> p j d", j=TT)
        xT = region("xT", 3072)[:, :].rearrange("p (k t) -> p k t", k=KD)
        R_O = region("branch_out", o_cols)
        R_Y = region("merge", y_cols)
        R_W = region("weight_ring", w_cols)
        R_A = region("arena", a_cols)
        R_M = region("small", m_cols)
        idx = ctx.enter_context(nc.sbuf_tensor("idx", [P, 8], I32))
        flag_i = ctx.enter_context(nc.sbuf_tensor("flag_i", [1, 1], I32))

        def cc(name, rows=P):
            o, w = CST[name]
            return cst[0:rows, o:o + w]
        ident = cc("ident")
        rope_t = cc("rope").rearrange("p (j c) -> p j c", j=TT)

        wring = R_W[:, :].rearrange("p (s k n) -> p s k n", s=NW, k=4)
        oT = R_O[:, :].rearrange("p (r k t) -> p r k t", r=3, k=4)

        A = Space(R_A, a_cols)
        fqT = A.take(4, T)
        mqT = A.take(4, T)
        fkT = A.take(4, T)
        fv_tok = A.take(TT, 512)
        qabsP = A.take(H, 256)
        qabsS = A.take(NB, P)
        qrP = A.take(H, 256)
        qrS = A.take(NB, P)
        mv_tok = A.take(2, 512)
        mkT = A.take(HM, 256)
        w_kv = A.take(1024)
        late = A.at
        w_q = A.take(2, 768)
        lat_raw = A.take(TT, 424)
        fk_tok = A.take(TT, 512)
        qn = A.take(TT, 256)
        qnT = A.take(2, T)
        mk_tok = A.take(2, 512)
        wukT = A.take(H, P)
        OE = Space(R_O, o_cols)
        mem_sb = OE.take(2, D)
        memT = OE.take(KD, 256)
        YE = Space(R_Y, y_cols)
        qn_up = YE.take(2, T)
        qr_tok = YE.take(TT, 256)
        qr_rot = YE.take(TT, 256)
        scr = YE.take(256)
        gq_b = YE.take(256)
        gkv_b = YE.take(128)
        B = Space(R_A, a_cols, late)
        fkc = B.take(2, 512)
        mkc = B.take(2, 512)
        fvc = [B.take(2, 512) for _ in range(2)]
        mvc = [B.take(2, 512) for _ in range(2)]
        fkTc = B.take(4, 256)
        mkTc = B.take(4, 256)
        L = Space(lngb, lngb_cols)
        latc = [L.take(2, KVL) for _ in range(2)]
        krc = [L.take(2, RD) for _ in range(2)]
        latTc = L.take(256)
        krTc = L.take(256)
        latn = L.take(TT, KVL)
        latT = L.take(T)
        Y = Space(R_Y, y_cols)
        prob = [Y.take(T) for _ in range(3)]
        pT = [Y.take(T) for _ in range(2)]
        qbd_fox = Y.take(640)
        olat = [Y.take(P) for _ in range(2)]
        M = Space(R_M, m_cols)
        krT = M.take(T)
        kr_rot = M.take(TT, RD)
        lf_new = M.take(TT, 8)
        LFn = M.take(TT, 40)
        b_f_b = M.take(8)
        ssq = M.take(6)
        rst = M.take(6)
        lft = M.take(4, 24)
        rt = M.take(3, 128)
        mark_fr = M.at
        FR = M.take(T)
        FX = M.take(256)
        LH = [M.take(256), Y.take(256)]
        qbd_mem = M.take(320)
        mx = M.take(len(U))
        sm = M.take(len(U))
        rs = M.take(len(U))
        C2 = Space(R_A, a_cols, B.at)
        lfc_raw = C2.take(16, 8)
        LFc = [C2.take(2, 40) for _ in range(2)]
        estage = R_A[:, a_cols - 512:a_cols]
        assert C2.at <= a_cols - 512
        G = Space(R_M, m_cols, mark_fr)
        egate = [G.take(512) for _ in range(2)]
        y = R_Y[:, :].rearrange("p (j d) -> p j d", j=TT)
        yT = R_O[:, 0:3072].rearrange("p (k t) -> p k t", k=KD)

        N = Space(R_Y, y_cols)
        w_rt = N.take(KD, E)
        rb_b = N.take(E)
        sc, sel, masked, rep, mask, tmp3 = (N.take(TT, E) for _ in range(6))
        g8 = N.take(24, 8)
        gs, gm = N.take(24), N.take(24)
        TGP = N.take(TT, (E + AHEAD + 1) * 3)
        tgp = TGP.rearrange("p j (e c) -> p j e c", c=3)
        t8 = N.take(TT, TOPK)
        wsum = N.take(TT)
        cmax = N.take(1)
        pcol = [N.take(TT, 3) for _ in range(2)]
        info = N.take(4, 2)
        empty = N.take(1)
        XO = Space(R_O, o_cols)
        xgT = [XO.take(KD, CAP) for _ in range(2)]
        sil = [XO.take(2, CAP) for _ in range(2)]
        hid = [XO.take(2, CAP) for _ in range(2)]
        onehot = [XO.take(TT, CAP) for _ in range(2)]
        xg = [R_M[:, mark_fr:mark_fr + D], lngb[:, 0:D], lngb[:, D:2 * D], R_W[:, 6144:6144 + D]]
        yo = [R_W[:, i * D:(i + 1) * D] for i in range(2)]
        SH = Space(R_O, o_cols)
        sh_sil, sh_up = SH.take(2, T), SH.take(2, T)
        ew = [R_A[:, i * 6144:(i + 1) * 6144] for i in range(4)]
        ew_gate = [v[:, 0:2048].rearrange("p (k f) -> p k f", k=KD) for v in ew]
        ew_up = [v[:, 2048:4096].rearrange("p (k f) -> p k f", k=KD) for v in ew]
        ew_down = [v[:, 4096:6144].rearrange("p (m n) -> p m n", m=2) for v in ew]
        sh_gate, sh_upw = (R_W[:, i * 2048:(i + 1) * 2048].rearrange("p (k f) -> p k f", k=KD) for i in range(2))
        sh_down = R_W[:, 4096:6144].rearrange("p (m n) -> p m n", m=2)
        gates_dram = nc.dram_tensor("gates", (6 * TT, P, 512), F32, kind="Internal").ap()
        x1_dram = nc.dram_tensor("x1_rows", (T, D), F32, kind="Internal").ap()
        sum_dram = nc.dram_tensor("sum", (T, D), F32, kind="Internal").ap()
        sum_rows = sum_dram.rearrange("(j p) d -> p j d", p=P)

        ps = {r: [ctx.enter_context(nc.psum_tensor(f"ps_{r}{i}", [P, 512], F32)) for i in range(2)] for r in "PSTV"}
        done = {r: sem(f"{r}_done") for r in "PSTV"}
        free = {r: sem(f"{r}_free") for r in "PSTV"}

        w_loaded = [sem(f"w_loaded{i}") for i in range(NW)]
        x_loaded = [sem(f"x_loaded{j}") for j in range(TT)]
        cst_loaded = sem("cst_loaded")
        mem_loaded = [sem(f"mem_loaded{j}") for j in range(2)]
        up_loaded = sem("up_loaded")
        vec_loaded = sem("vec_loaded")
        logf_loaded = sem("logf_loaded")
        kcache = {k: sem(f"{k}_cache") for k in ("fk", "mk")}
        vcache = {k: [sem(f"{k}_cache{i}") for i in range(2)] for k in ("lat", "fv", "mv")}
        ln_loaded = sem("ln_loaded")
        stored = sem("stored")
        dve_step = sem("dve_step")
        act_step = sem("act_step")
        sq_ready = sem("sq_ready")
        rstd_ready = sem("rstd_ready")
        nz_ready = sem("nz_ready")
        lse_ready = sem("lse_ready")
        lat_ready = sem("lat_ready")
        logf_ready = sem("logf_ready")
        qrope_ready = sem("qrope_ready")
        prep_ready = sem("prep_ready")
        max_ready = sem("max_ready")
        exp_ready = sem("exp_ready")
        norm_ready = sem("norm_ready")
        lnv_ready = sem("lnv_ready")
        rstd1_ready = sem("rstd1_ready")
        x1_ready = sem("x1_ready")
        y_out = sem("y_out")
        x1_stored = sem("x1_stored")
        router_loaded = sem("router_loaded")
        ln2_loaded = sem("ln2_loaded")
        z_ready = sem("z_ready")
        gates_stored = sem("gates_stored")
        gate_ready = sem("gate_ready")
        gates_loaded = [sem(f"gates_loaded{i}") for i in range(2)]
        ez_ready = sem("ez_ready")
        mask_ready = sem("mask_ready")
        count_ready = sem("count_ready")
        flag_ready = sem("flag_ready")
        hidden_ready = sem("hidden_ready")
        gate_up_loaded = [sem(f"gate_up_loaded{i}") for i in range(4)]
        down_loaded = [sem(f"down_loaded{i}") for i in range(4)]
        onehot_built = sem("onehot_built")
        slots_done = sem("slots_done")
        idx_ready = sem("idx_ready")
        info_ready = sem("info_ready")
        row_buffer_free = sem("row_buffer_free")
        dst_ready = sem("dst_ready")
        empty_found = sem("empty_found")
        scatters_started = sem("scatters_started")
        column_copied = sem("column_copied")
        gathers_started = sem("gathers_started")
        xg_loaded = [sem(f"xg_loaded{i}") for i in range(4)]
        xg_cleared = sem("xg_cleared")
        xg_turned = sem("xg_turned")
        xgT_ready = sem("xgT_ready")
        gate_done = sem("gate_done")
        gate_up_done = sem("gate_up_done")
        silu_ready = sem("silu_ready")
        hid_ready = sem("hid_ready")
        down_done = sem("down_done")
        down_free = sem("down_free")
        rows_stored = [sem(f"rows_stored{i}") for i in range(4)]
        all_written = sem("all_written")
        overflow_step = sem("overflow_step")
        sum_begun, sum_loaded = sem("sum_begun"), sem("sum_loaded")
        out_ready = sem("out_ready")

        d_of = {
            "lat": a["w_in"][0], "in": a["w_in"][0], "mem_k": a["w_mem_k"][0], "mem_v": a["w_mem_v"][0],
            "br_mla": a["w_br_mla"][0], "br_fox": a["w_br_fox"][0], "br_mem": a["w_br_mem"][0], "out": a["w_out"][0],
        }

        def rowblocks(m, k0, nk, c0, n):
            return m[k0 * P:(k0 + nk) * P, c0:c0 + n].rearrange("(k p) n -> p k n", p=P)

        def unit_stage(n):
            return U[n][4], U[n][5] // P

        def rounds(eng, body):
            body(0)
            eng.wait_ge(flag_ready, 1)
            most = eng.value_load(flag_i[0:1, 0:1], min_val=0, max_val=T)
            for r in range(1, ROUNDS):
                with eng.If(most > r * CAP):
                    body(r)

        block = ctx.enter_context(nc.Block())

        def w_load(eng, n):
            name, k0, c0, w = WU[n] if len(WU[n]) == 4 else WU[n] + (0, 0, 0)
            if n >= NW:
                ring = last_use[n - NW][0]
                eng.wait_ge(done[ring], done_at(*last_use[n - NW]))
            s = n % NW
            if n >= first_of["s_gate"]:
                dst, src = ((sh_gate, rowblocks(a["w_s_gate"][0], 0, KD, 0, FE)), (sh_upw, rowblocks(a["w_s_up"][0], 0, KD, 0, FE)),
                            (sh_down, rowblocks(a["w_s_down"][0], 0, 2, 0, D)))[n - first_of["s_gate"]]
                eng.dma_start(dst, src).then_inc(w_loaded[s], 16)
                return
            eng.dma_start(wring[:, s, :, 0:w], rowblocks(d_of[name], k0, 4, c0, w)).then_inc(w_loaded[s], 16)
            if name == "lat":
                eng.dma_start(wring[:, s, :, 416:424],
                             rowblocks(d_of[name], k0, 4, OFF["fl"], 8)).then_inc(w_loaded[s], 16)

        @block.sync
        def _(sp):
            def load_expert(r, i, q):
                e = i * 4 + q
                if r or not isinstance(i, int):
                    sp.wait_ge(gate_up_done, E * r + e - 3)
                sp.dma_start(ew_gate[q], w_eg[bass.ds(e, 1)].rearrange("e (p k) f -> p (e k) f", p=P)).then_inc(gate_up_loaded[q], 16)
                sp.dma_start(ew_up[q], w_eu[bass.ds(e, 1)].rearrange("e (p k) f -> p (e k) f", p=P)).then_inc(gate_up_loaded[q], 16)
                if r or not isinstance(i, int):
                    sp.wait_ge(down_done, 2 * (E * r + e - 3))
                sp.dma_start(ew_down[q], w_ed[bass.ds(e, 1)].rearrange("e (m p) n -> p (e m) n", p=P)).then_inc(down_loaded[q], 16)

            w_eg, w_eu, w_ed = a["w_e_gate"][0], a["w_e_up"][0], a["w_e_down"][0]
            xs = [a["x_prompt"][0, 0:P], a["x_prompt"][0, P:2 * P], a["x_sample"].rearrange("b s d -> (b s) d")]
            sp.dma_start(cst[:, :], a["consts"]).then_inc(cst_loaded, 16)
            for j in range(TT):
                sp.dma_start(x_sb[:, j, :], xs[j]).then_inc(x_loaded[j], 16)
            w_load(sp, 0)
            w_load(sp, 1)
            for t, v, n in ((gq_b, "q_norm_g", 256), (gkv_b, "kv_norm_g", 128), (b_f_b, "b_f", 8)):
                sp.dma_start(t, a[v].to_broadcast([P, n])).then_inc(vec_loaded, 16)
            for j in range(2):
                sp.dma_start(mem_sb[:, j, :], a["mem_prompt"][0, j * P:(j + 1) * P]).then_inc(mem_loaded[j], 16)
            sp.dma_start(w_kv, a["w_kv_up"][0]).then_inc(up_loaded, 16)
            w_load(sp, 2)
            w_load(sp, 3)
            sp.dma_start(w_q, rowblocks(a["w_q_up"][0], 0, 2, 0, 768)).then_inc(up_loaded, 16)
            for n in range(4, 14):
                w_load(sp, n)
            for n in range(14, 14 + NW):
                w_load(sp, n)

            def wait_unit(kind, b, ring):
                n = next(i for i, u in enumerate(U) if u[:3] == (kind, "s", b))
                sp.wait_ge(done[ring], done_at("V", "o", n))
            sp.wait_ge(done["T"], done_at("T", "mk", 1))
            sp.wait_ge(done["P"], done_at("P", "mv", 1))
            sp.wait_ge(stored, 16 * PROJ_STORES)
            sp.wait_ge(free["V"], done_at("V", "c", "p"))
            sp.dma_start(lfc_raw, a["cache_fox_logf"][0].rearrange("b (t p) h -> p (b t) h", p=P)).then_inc(logf_loaded, 16)
            for b in range(NB):
                if b >= 2:
                    wait_unit("mla", b - 2, "V")
                sp.dma_start(latc[b % 2], a["cache_mla_latent"][0, b].rearrange("(t p) c -> p t c", p=P)).then_inc(vcache["lat"][b % 2], 16)
                sp.dma_start(krc[b % 2], a["cache_mla_krope"][0, b].rearrange("(t p) c -> p t c", p=P)).then_inc(vcache["lat"][b % 2], 16)
                if b >= 1:
                    sp.wait_ge(done["T"], done_at("T", "cfk", b - 1, 1))
                sp.dma_start(fkc, a["cache_fox_k"][0, b].rearrange("(t p) h c -> p t (h c)", p=P)).then_inc(kcache["fk"], 16)
                if b >= 2:
                    wait_unit("fox", b - 2, "V")
                sp.dma_start(fvc[b % 2], a["cache_fox_v"][0, b].rearrange("(t p) h c -> p t (h c)", p=P)).then_inc(vcache["fv"][b % 2], 16)
                if b >= 1:
                    sp.wait_ge(done["T"], done_at("T", "cmk", b - 1, 1))
                sp.dma_start(mkc, a["cache_mem_k"][0, b].rearrange("(t p) h c -> p t (h c)", p=P)).then_inc(kcache["mk"], 16)
                if b >= 2:
                    wait_unit("mem", b - 2, "V")
                sp.dma_start(mvc[b % 2], a["cache_mem_v"][0, b].rearrange("(t p) h c -> p t (h c)", p=P)).then_inc(vcache["mv"][b % 2], 16)
            for n in range(first_of["br"], len(WU)):
                w_load(sp, n)
                if n in (30, 32, 34, 35):
                    load_expert(0, 0, (30, 32, 34, 35).index(n))
                if n == 29:
                    sp.wait_ge(done["V"], done_at("V", "b", 0, 0, 0))
                    sp.dma_start(lngb[:, 0:D], a["ln1_g"].to_broadcast([P, D])).then_inc(ln_loaded, 16)
                    sp.dma_start(lngb[:, D:2 * D], a["ln1_b"].to_broadcast([P, D])).then_inc(ln_loaded, 16)
            sp.wait_ge(free["T"], done_at("T", "y", 2, 1))
            sp.wait_ge(done["T"], done_at("T", "y", 2, 1))
            sp.dma_start(w_rt, rowblocks(a["w_router"][0], 0, KD, 0, E)).then_inc(router_loaded, 16)
            sp.dma_start(rb_b, a["router_bias"].to_broadcast([P, E])).then_inc(router_loaded, 16)
            sp.wait_ge(x1_ready, TT)
            sp.dma_start(x1_dram.rearrange("(j p) d -> p j d", p=P), x_sb).then_inc(x1_stored, 16)

            def expert_round(r):
                if r:
                    for q in range(4):
                        load_expert(r, 0, q)
                with sp.Fori(1, E // 4) as i:
                    for q in range(4):
                        load_expert(r, i, q)
            rounds(sp, expert_round)
            sp.wait_ge(all_written, 1)
            sp.dma_start(x_sb, sum_rows).then_inc(sum_loaded, 16)
            sp.dma_start(lngb[:, 0:D], a["ln2_g"].to_broadcast([P, D])).then_inc(ln2_loaded, 16)
            sp.dma_start(lngb[:, D:2 * D], a["ln2_b"].to_broadcast([P, D])).then_inc(ln2_loaded, 16)
            sp.wait_ge(out_ready, TT)
            sp.dma_start(outs["y_prompt"][0].rearrange("(j p) d -> p j d", p=P), x_sb[:, 0:2, :]).then_inc(y_out, 16)
            sp.dma_start(outs["y_sample"].rearrange("b s d -> (b s) d"), x_sb[:, 2, :]).then_inc(y_out, 16)
            sp.wait_ge(y_out, 32)

        def store_pair(eng, name, src):
            eng.dma_start(flat_out("p_" + name, 2), src[:, 0:2, :]).then_inc(stored, 16)
            eng.dma_start(flat_out("s_" + name, 1), src[:, 2:3, :]).then_inc(stored, 16)

        def flat_out(name, nj):
            o = outs[name]
            nd = len(o.shape)
            if nd == 4:
                return o.rearrange("o b s c -> (o b s) c").rearrange("(j p) c -> p j c", p=P)
            return o.rearrange("o b s h c -> (o b s) (h c)").rearrange("(j p) c -> p j c", p=P)

        @block.gpsimd
        def _(pool):
            pool.wait_ge(lat_ready, 1)
            store_pair(pool, "mla_latent", latn)
            store_pair(pool, "mla_krope", kr_rot)
            pool.wait_ge(logf_ready, 1)
            store_pair(pool, "fox_logf", lf_new)
            pool.wait_ge(free["P"], done_at("P", "fk", 2))
            store_pair(pool, "fox_k", fk_tok)
            pool.wait_ge(free["P"], done_at("P", "fv", 2))
            store_pair(pool, "fox_v", fv_tok)
            pool.wait_ge(free["P"], done_at("P", "mk", 1))
            pool.dma_start(flat_out("p_mem_k", 2), mk_tok).then_inc(stored, 16)
            pool.wait_ge(free["P"], done_at("P", "mv", 1))
            pool.dma_start(flat_out("p_mem_v", 2), mv_tok).then_inc(stored, 16)
            pool.wait_ge(stored, 16 * PROJ_STORES)
            pool.wait_ge(x1_stored, 16)

            for q in range(4):
                last = nc.gpsimd.memset(xg[q][0:CAP, :], 0.0)
            last.then_inc(xg_cleared, 1)
            pool.wait_ge(xg_cleared, 1)

            def gather(r, e, q):
                pool.wait_ge(idx_ready, (E + AHEAD) * r + e + 1)
                pool.sem_inc(gathers_started, 1)
                pool.indirect_dma_start(xg[q][0:CAP, :], None, x1_dram, bass.IndirectOffsetOnAxis(ap=idx[0:CAP, q:q + 1], axis=0),
                                        bounds_check=T - 1, oob_is_err=False).then_inc(xg_loaded[q], 16)

            def scatter(r, e, q):
                pool.wait_ge(down_free, 2 * (E * r + e + 2))
                pool.wait_ge(dst_ready, E * r + e + 1)
                pool.sem_inc(scatters_started, 1)
                pool.indirect_dma_start(sum_dram, bass.IndirectOffsetOnAxis(ap=idx[0:CAP, 4 + q:5 + q], axis=0), yo[q % 2][0:CAP, :], None,
                                        bounds_check=T - 1, oob_is_err=False, compute_op=ALU.add).then_inc(rows_stored[q], 16)

            def stored_rows(r, i, q):
                pool.wait_ge(rows_stored[q], 16 * ((E // 4) * r + i + 1))
                pool.sem_inc(row_buffer_free, 1)

            def expert_round(r):
                for e in range(AHEAD):
                    gather(r, e, e)
                with pool.Fori(0, E // 4) as i:
                    for q in range(4):
                        gather(r, i * 4 + q + AHEAD, (q + AHEAD) % 4)
                        scatter(r, i * 4 + q, q)
                        stored_rows(r, i, q)
                for q in range(4):
                    pool.wait_ge(xg_loaded[q], 16 * GATHERS[q] * (r + 1))
            pool.sem_inc(row_buffer_free, 2)
            pool.wait_ge(sum_begun, 16)
            rounds(pool, expert_round)
            pool.sem_inc(all_written, 1)

        @block.tensor
        def _(pe):
            mm = nc.tensor.matmul

            def bank(st):
                n = pos_in[st]
                if n >= 2:
                    pe.wait_ge(free[st[0]], n - 1)
                return ps[st[0]][n % 2]

            def w_wait(n):
                s = n % NW
                per = [32 if WU[m][0] == "lat" else 16 for m in range(n + 1) if m % NW == s]
                pe.wait_ge(w_loaded[s], sum(per))
                return wring[:, s]

            def tr(out, in_, n):
                return nc.tensor.transpose(out, in_, ident[0:n, 0:n])

            def tok_major(st, first, src, j, w):
                out = bank(st)
                for k in range(KD):
                    if k % 4 == 0:
                        slot = w_wait(first + k // 4)
                    last = mm(out[:, 0:w], src[:, k, j * P:(j + 1) * P], slot[:, k % 4, 0:w], start=(k == 0), stop=(k == KD - 1))
                last.then_inc(done["P"], 1)

            def feat_major(st, first, m):
                out = bank(st)
                for k in range(KD):
                    if k % 4 == 0:
                        slot = w_wait(first + k // 4)
                    last = mm(out[:, 0:T], slot[:, k % 4, m * P:(m + 1) * P], xT[:, k, :], start=(k == 0), stop=(k == KD - 1))
                last.then_inc(done["P"], 1)

            def scores(n):
                kind, g, i, q, rows, keys = U[n]
                pe.wait_ge(prep_ready, n + 1)
                out = bank(("S", n))
                if g == "p":
                    qs = slice(q * P, (q + 1) * P)
                    if kind == "mla":
                        mm(out[:, 0:keys], qabsP[:, i, qs], latT[:, 0:keys], start=True, stop=False)
                        mm(out[:, 0:keys], qrP[0:RD, i, qs], krT[0:RD, 0:keys], start=False, stop=False)
                        last = mm(out[:, keys - P:keys], ident, cc("chunk"), start=False, stop=True)
                    elif kind == "fox":
                        h0 = (i % 2) * 64
                        mm(out[:, 0:keys], fqT[h0:h0 + 64, i // 2, qs], fkT[h0:h0 + 64, i // 2, 0:keys], start=True, stop=False)
                        mm(out[:, 0:keys], LH[i % 2][:, qs], FR[:, 0:keys], start=False, stop=False)
                        last = mm(out[:, keys - P:keys], ident, cc("causal"), start=False, stop=True)
                    else:
                        last = mm(out[:, 0:keys], mqT[:, i, qs], mkT[:, i, :], start=True, stop=True)
                elif kind == "mla":
                    mm(out[:, 0:PAST], qabsS[:, i, :], latTc, start=True, stop=False)
                    mm(out[:, 0:PAST], qrS[0:RD, i, :], krTc[0:RD, :], start=False, stop=False)
                    mm(out[:, PAST:keys], qabsS[:, i, :], latT[:, 256:T], start=False, stop=False)
                    mm(out[:, PAST:keys], qrS[0:RD, i, :], krT[0:RD, 256:T], start=False, stop=False)
                    w0 = (7 - i) * NQ
                    last = mm(out[:, PAST:keys], ident, cc("wmla")[:, w0:w0 + P], start=False, stop=True)
                elif kind == "fox":
                    for m in range(4):
                        mm(out[:, 0:PAST], qbd_fox[:, m * P:(m + 1) * P], fkTc[:, m, :], start=(m == 0), stop=False)
                    for m in range(4):
                        mm(out[:, PAST:keys], qbd_fox[:, m * P:(m + 1) * P], fkT[:, m, 256:T], start=False, stop=False)
                    mm(out[:, 0:keys], LH[0][:, 0:P], FR[:, :], start=False, stop=False)
                    w0 = (7 - i) * NQ
                    last = mm(out[:, PAST:keys], ident, cc("wfox")[:, w0:w0 + P], start=False, stop=True)
                else:
                    for m in range(HM):
                        last = mm(out[0:64, 0:keys], qbd_mem[:, m * 64:(m + 1) * 64], mkTc[:, m, :], start=(m == 0), stop=(m == HM - 1))
                last.then_inc(done["S"], 1)

            def values(n):
                kind, g, i, q, rows, keys = U[n]
                pe.wait_ge(free["T"], done_at("T", "p", n))
                out = bank(("V", "o", n))
                pt = pT[n % 2]
                nk = keys // P
                if kind == "mla":
                    for t in range(nk):
                        if g == "p":
                            v = latn[:, t, :]
                        else:
                            v = latc[i % 2][:, t, :] if t < 2 else latn[:, 2, :]
                        last = mm(out[:, 0:P], v, pt[:, t * P:(t + 1) * P], start=(t == 0), stop=(t == nk - 1))
                elif kind == "fox" and g == "p":
                    h0 = (i % 2) * 64
                    for t in range(nk):
                        last = mm(out[h0:h0 + 64, 0:P], fv_tok[:, t, i * 64:(i + 1) * 64], pt[:, t * P:(t + 1) * P],
                                  start=(t == 0), stop=(t == nk - 1))
                elif kind == "fox":
                    pe.wait_ge(vcache["fv"][i % 2], 16 * (i // 2 + 1))
                    for m in range(4):
                        for t in range(nk):
                            v = fvc[i % 2][:, t, m * P:(m + 1) * P] if t < 2 else fv_tok[:, 2, m * P:(m + 1) * P]
                            last = mm(out[:, m * 32:(m + 1) * 32], v, pt[:, t * P + m * 32:t * P + (m + 1) * 32],
                                      start=(t == 0), stop=(t == nk - 1))
                elif g == "p":
                    for t in range(nk):
                        last = mm(out[:, 0:P], mv_tok[:, t, i * P:(i + 1) * P], pt[:, t * P:(t + 1) * P],
                                  start=(t == 0), stop=(t == nk - 1))
                else:
                    pe.wait_ge(vcache["mv"][i % 2], 16 * (i // 2 + 1))
                    for m in range(HM):
                        for t in range(nk):
                            last = mm(out[:, m * NQ:(m + 1) * NQ], mvc[i % 2][:, t, m * P:(m + 1) * P],
                                      pt[:, t * P + m * NQ:t * P + (m + 1) * NQ], start=(t == 0), stop=(t == nk - 1))
                last.then_inc(done["V"], 1)

            def gate_products(n, k0):
                st = ("P", "g", n)
                out = bank(st) if k0 == 0 else ps["P"][pos_in[st] % 2]
                slot = w_wait(first_of["g"] + (n // TT) * 2 + k0 // 4)
                j = n % TT
                for k in (k0, k0 + 1):
                    last = mm(out[:, :], xT[:, k, j * P:(j + 1) * P], slot[:, k % 4, :], start=(k == 0), stop=(k == KD - 1))
                if k0 == KD - 2:
                    last.then_inc(done["P"], 1)

            pe.wait_ge(cst_loaded, 16)
            for st in PLAN:
                ring, key = st[0], st[1:]
                if ring == "T":
                    if key[0] == "x":
                        _, j, half = key
                        pe.wait_ge(x_loaded[j], 16)
                        out = bank(st)
                        for k in range(4):
                            kk = half * 4 + k
                            last = tr(out[:, k * P:(k + 1) * P], x_sb[:, j, kk * P:(kk + 1) * P], P)
                    elif key[0] == "mem":
                        _, j, half = key
                        pe.wait_ge(mem_loaded[j], 16)
                        out = bank(st)
                        for k in range(4):
                            kk = half * 4 + k
                            last = tr(out[:, k * P:(k + 1) * P], mem_sb[:, j, kk * P:(kk + 1) * P], P)
                    elif key[0] == "uk":
                        pe.wait_ge(up_loaded, 32)
                        out = bank(st)
                        for k in range(4):
                            h = key[1] * 4 + k
                            last = tr(out[0:64, k * P:(k + 1) * P], w_kv[:, h * P:h * P + 64], P)
                    elif key[0] == "lat":
                        j = key[1]
                        pe.wait_ge(lat_ready, 1)
                        out = bank(st)
                        tr(out[:, 0:P], qn[:, j, 0:P], P)
                        tr(out[:, P:2 * P], qn[:, j, P:2 * P], P)
                        tr(out[:, 2 * P:3 * P], latn[:, j, :], P)
                        last = tr(out[0:RD, 3 * P:4 * P], kr_rot[:, j, :], P)
                    elif key[0] == "qr":
                        _, j, half = key
                        pe.wait_ge(qrope_ready, j + 1)
                        out = bank(st)
                        for k in range(4):
                            h = half * 4 + k
                            last = tr(out[0:RD, k * P:(k + 1) * P], qr_rot[:, j, h * RD:(h + 1) * RD], P)
                    elif key[0] == "fk":
                        j = key[1]
                        pe.wait_ge(free["P"], done_at("P", "fk", j))
                        out = bank(st)
                        for m in range(4):
                            last = tr(out[:, m * P:(m + 1) * P], fk_tok[:, j, m * P:(m + 1) * P], P)
                    elif key[0] == "mk":
                        j = key[1]
                        pe.wait_ge(free["P"], done_at("P", "mk", j))
                        out = bank(st)
                        for m in range(4):
                            last = tr(out[:, m * P:(m + 1) * P], mk_tok[:, j, m * P:(m + 1) * P], P)
                    elif key[0] == "clat":
                        b = key[1]
                        pe.wait_ge(vcache["lat"][b % 2], 32 * (b // 2 + 1))
                        out = bank(st)
                        for t in range(2):
                            tr(out[:, t * P:(t + 1) * P], latc[b % 2][:, t, :], P)
                            last = tr(out[0:RD, (2 + t) * P:(3 + t) * P], krc[b % 2][:, t, :], P)
                    elif key[0] in ("cfk", "cmk"):
                        _, b, t = key
                        src = fkc if key[0] == "cfk" else mkc
                        pe.wait_ge(kcache[key[0][1:]], 16 * (b + 1))
                        out = bank(st)
                        for m in range(4):
                            last = tr(out[:, m * P:(m + 1) * P], src[:, t, m * P:(m + 1) * P], P)
                    elif key[0] == "p":
                        n = key[1]
                        rows, nk = unit_stage(n)
                        pe.wait_ge(norm_ready, n + 1)
                        out = bank(st)
                        for t in range(nk):
                            last = tr(out[:, t * P:t * P + rows], prob[n % 3][0:rows, t * P:(t + 1) * P], rows)
                    elif key[0] == "y":
                        _, j, half = key
                        pe.wait_ge(free["V"], done_at("V", "b", 2, 1, 2))
                        out = bank(st)
                        for k in range(4):
                            kk = half * 4 + k
                            last = tr(out[:, k * P:(k + 1) * P], y[:, j, kk * P:(kk + 1) * P], P)
                    elif key[0] == "x1":
                        _, j, half = key
                        pe.wait_ge(x1_ready, j + 1)
                        out = bank(st)
                        for k in range(4):
                            kk = half * 4 + k
                            last = tr(out[:, k * P:(k + 1) * P], x_sb[:, j, kk * P:(kk + 1) * P], P)
                    last.then_inc(done["T"], 1)
                elif ring == "P":
                    if key[0] == "lat":
                        pe.wait_ge(free["T"], done_at("T", "x", key[1], 1))
                        tok_major(st, first_of["lat"], xT, key[1], 424)
                    elif key[0] in ("fk", "fv"):
                        tok_major(st, first_of[key[0]], xT, key[1], 512)
                    elif key[0] in ("mk", "mv"):
                        pe.wait_ge(free["T"], done_at("T", "mem", 1, 1))
                        tok_major(st, first_of[key[0]], memT, key[1], 512)
                    elif key[0] in ("fq", "mq"):
                        feat_major(st, first_of[key[0]], key[1])
                    elif key[0] == "qr":
                        j = key[1]
                        pe.wait_ge(free["T"], done_at("T", "lat", j))
                        pe.wait_ge(up_loaded, 32)
                        out = bank(st)
                        for k in range(2):
                            wv = w_q[:, k, :].rearrange("p (h c) -> p h c", h=H)[:, :, ND:ND + RD]
                            last = mm(out[:, 0:256], qnT[:, k, j * P:(j + 1) * P], wv, start=(k == 0), stop=(k == 1))
                        last.then_inc(done["P"], 1)
                    elif key[0] == "qn":
                        h = key[1]
                        out = bank(st)
                        for k in range(2):
                            last = mm(out[0:64, 0:T], w_q[:, k, h * 96:h * 96 + 64], qnT[:, k, :], start=(k == 0), stop=(k == 1))
                        last.then_inc(done["P"], 1)
                    elif key[0] == "qa":
                        h = key[1]
                        pe.wait_ge(free["P"], done_at("P", "qn", h))
                        pe.wait_ge(free["T"], done_at("T", "uk", 1))
                        out = bank(st)
                        mm(out[:, 0:T], wukT[0:64, h, :], qn_up[0:64, h % 2, :], start=True, stop=True).then_inc(done["P"], 1)
                    elif key[0] == "g":
                        gate_products(key[1], KD - 2)
                    elif key[0] == "sh":
                        m = key[1]
                        pe.wait_ge(free["T"], done_at("T", "x1", 2, 1))
                        w_wait(first_of["s_gate"] + m // 2)
                        out = bank(st)
                        wv = (sh_gate, sh_upw)[m // 2]
                        for k in range(KD):
                            last = mm(out[:, 0:T], wv[:, k, (m % 2) * P:(m % 2 + 1) * P], xT[:, k, :], start=(k == 0), stop=(k == KD - 1))
                        last.then_inc(done["P"], 1)
                elif ring == "gpiece":
                    gate_products(*key)
                elif ring == "S":
                    n = key[0]
                    scores(n)
                elif ring == "V":
                    if key[0] == "c":
                        out = bank(st)
                        if key[1] == "p":
                            pe.wait_ge(logf_ready, 1)
                            mm(out[0:40, 0:256], LFn[:, 0, :], cst[:, CST["tri"][0]:CST["tri"][0] + 256], start=True, stop=False)
                            last = mm(out[0:40, P:256], LFn[:, 1, :], cc("tri"), start=False, stop=True)
                        else:
                            b = key[1]
                            n = next(i for i, u in enumerate(U) if u[:3] == ("fox", "s", b))
                            pe.wait_ge(prep_ready, n)
                            t0 = CST["tri"][0]
                            mm(out[0:40, 0:T], LFc[b % 2][:, 0, :], cst[:, t0:t0 + T], start=True, stop=False)
                            mm(out[0:40, P:T], LFc[b % 2][:, 1, :], cst[:, t0:t0 + 256], start=False, stop=False)
                            last = mm(out[0:40, 256:T], LFn[:, 2, :], cc("blk"), start=False, stop=True)
                        last.then_inc(done["V"], 1)
                    elif key[0] == "o":
                        values(key[1])
                    elif key[0] == "ov":
                        kind, g, i, q, rows, keys = U[key[1]]
                        pe.wait_ge(free["V"], done_at("V", "o", key[1]))
                        out = bank(st)
                        if g == "p":
                            h0 = (i % 2) * 64
                            last = mm(out[h0:h0 + 64, 0:P], w_kv[:, i * P + 64:(i + 1) * P], olat[key[1] % 2], start=True, stop=True)
                        else:
                            for h in range(H):
                                h0 = (h % 2) * 64
                                last = mm(out[h0:h0 + 64, (h // 2) * NQ:(h // 2 + 1) * NQ], w_kv[:, h * P + 64:(h + 1) * P],
                                          olat[key[1] % 2][:, h * NQ:(h + 1) * NQ], start=True, stop=True)
                        last.then_inc(done["V"], 1)
                    elif key[0] == "b":
                        _, br, cb, j = key
                        pe.wait_ge(free["V"], done_at("V", "o", len(U) - 1))
                        slot = w_wait(first_of["br"] + br * 2 + cb)
                        out = bank(st)
                        for k in range(4):
                            last = mm(out[:, :], oT[:, br, k, j * P:(j + 1) * P], slot[:, k, :], start=(k == 0), stop=(k == 3))
                        last.then_inc(done["V"], 1)
                    elif key[0] == "out":
                        _, j, half = key
                        pe.wait_ge(free["T"], done_at("T", "y", j, 1))
                        out = bank(st)
                        for k in range(KD):
                            if k % 4 == 0:
                                slot = w_wait(first_of["out"] + half * 2 + k // 4)
                            last = mm(out[:, :], yT[:, k, j * P:(j + 1) * P], slot[:, k % 4, :], start=(k == 0), stop=(k == KD - 1))
                        last.then_inc(done["V"], 1)
                    elif key[0] == "router":
                        j = key[1]
                        pe.wait_ge(free["T"], done_at("T", "x1", 2, 1))
                        pe.wait_ge(router_loaded, 32)
                        out = bank(st)
                        for k in range(KD):
                            last = mm(out[:, 0:E], xT[:, k, j * P:(j + 1) * P], w_rt[:, k, :], start=(k == 0), stop=(k == KD - 1))
                        last.then_inc(done["V"], 1)
                    elif key[0] == "pos":
                        j = key[1]
                        pe.wait_ge(mask_ready, 1)
                        out = bank(st)
                        for jj in range(j):
                            mm(out[:, 0:E], cc("ones")[:, 0:P], mask[:, jj, :], start=(jj == 0), stop=False)
                        mm(out[:, 0:E], cc("strict"), mask[:, j, :], start=(j == 0), stop=True).then_inc(done["V"], 1)
                    elif key[0] == "flag":
                        pe.wait_ge(count_ready, 1)
                        tr(bank(st)[0:1, 0:P], cmax, P).then_inc(done["V"], 1)
                    elif key[0] == "shd":
                        _, j, half = key
                        pe.wait_ge(hidden_ready, 1)
                        w_wait(first_of["s_down"])
                        out = bank(st)
                        for m in range(2):
                            last = mm(out[:, :], sh_sil[:, m, j * P:(j + 1) * P], sh_down[:, m, half * 512:(half + 1) * 512],
                                      start=(m == 0), stop=(m == 1))
                        last.then_inc(done["V"], 1)

            def slot_tokens(r, e, par):
                pe.wait_ge(onehot_built, (E + AHEAD + 1) * r + e + 1)
                for j in range(TT):
                    last = mm(ps["S"][par][0:CAP, 0:2], onehot[par][:, j, :], pcol[par][:, j, 0:2], start=(j == 0), stop=(j == TT - 1))
                last.then_inc(slots_done, 1)

            def turn(r, e, count, q):
                pe.wait_ge(xg_loaded[q], 16 * (GATHERS[q] * r + count + 1))
                xv = xg[q][0:CAP, :].rearrange("c (d k) -> c k d", k=KD)
                for half in range(2):
                    for k in range(4):
                        last = nc.tensor.transpose(ps["T"][half][:, k * CAP:(k + 1) * CAP], xv[:, half * 4 + k, :], ident[0:CAP, 0:CAP])
                    last.then_inc(xg_turned, 1)

            def expert(r, i, q):
                e, par = i * 4 + q, q % 2
                pe.wait_ge(gate_up_loaded[q], 32 * ((E // 4) * r + i + 1))
                pe.wait_ge(xgT_ready, 2 * ((E + 1) * r + e + 1))
                for m in range(4):
                    wv = (ew_gate, ew_up)[m // 2][q]
                    for k in range(KD):
                        last = mm(ps["P"][m // 2][:, (m % 2) * CAP:(m % 2 + 1) * CAP], wv[:, k, (m % 2) * P:(m % 2 + 1) * P], xgT[par][:, k, :],
                                  start=(k == 0), stop=(k == KD - 1))
                    if m == 1:
                        last.then_inc(gate_done, 1)
                last.then_inc(gate_up_done, 1)
                turn(r, e + 1, i + (q + 1) // 4, (q + 1) % 4)
                slot_tokens(r, e + AHEAD, 1 - par)
                pe.wait_ge(down_loaded[q], 16 * ((E // 4) * r + i + 1))
                pe.wait_ge(hid_ready, E * r + e + 1)
                pe.wait_ge(down_free, 2 * (E * r + e + 1))
                for half in range(2):
                    for m in range(2):
                        last = mm(ps["V"][half][0:CAP, :], hid[par][:, m, :], ew_down[q][:, m, half * 512:(half + 1) * 512],
                                  start=(m == 0), stop=(m == 1))
                    last.then_inc(down_done, 1)

            def expert_round(r):
                for e in range(AHEAD):
                    slot_tokens(r, e, e % 2)
                turn(r, 0, 0, 0)
                with pe.Fori(0, E // 4) as i:
                    for q in range(4):
                        expert(r, i, q)
            for ring in "PTV":
                pe.wait_ge(free[ring], count[ring])
            rounds(pe, expert_round)

        @block.scalar
        def _(act):
            chain = [0]

            def link(ins):
                chain[0] += 1
                ins.then_inc(act_step, 1)
                act.wait_ge(act_step, chain[0])

            gates = {"made": 0, "stored": 0}

            def store_gates():
                n = gates["stored"]
                if n < gates["made"]:
                    act.wait_ge(gate_ready, n + 1)
                    act.dma_start(gates_dram[n], estage).then_inc(gates_stored, 16)
                    gates["stored"] += 1

            fn = nc.scalar.activation
            act.wait_ge(cst_loaded, 16)
            one = cc("ones")[:, 0:1]
            eps = cc("eps")
            for st in PLAN:
                ring, key = st[0], st[1:]
                if ring == "P":
                    act.wait_ge(done["P"], done_at(*st))
                    src = ps["P"][pos_in[st] % 2]
                    if key[0] == "lat":
                        last = fn(lat_raw[:, key[1], :], src[:, 0:424], ACT.Copy)
                    elif key[0] == "fk":
                        last = fn(fk_tok[:, key[1], :], src[:, :], ACT.Copy)
                    elif key[0] == "fv":
                        last = fn(fv_tok[:, key[1], :], src[:, :], ACT.Copy)
                    elif key[0] == "fq":
                        last = fn(fqT[:, key[1], :], src[:, 0:T], ACT.Copy, scale=FOX_SCALE)
                    elif key[0] == "mq":
                        last = fn(mqT[:, key[1], :], src[:, 0:T], ACT.Copy, scale=MEM_SCALE)
                    elif key[0] == "mk":
                        last = fn(mk_tok[:, key[1], :], src[:, :], ACT.Copy)
                    elif key[0] == "mv":
                        last = fn(mv_tok[:, key[1], :], src[:, :], ACT.Copy)
                    elif key[0] == "qr":
                        last = fn(qr_tok[:, key[1], :], src[:, 0:256], ACT.Copy, scale=MLA_SCALE)
                    elif key[0] == "qn":
                        h = key[1]
                        if h >= 2:
                            act.wait_ge(done["P"], done_at("P", "qa", h - 2))
                        last = fn(qn_up[0:64, h % 2, :], src[0:64, 0:T], ACT.Copy)
                    elif key[0] == "qa":
                        h = key[1]
                        fn(qabsP[:, h, :], src[:, 0:256], ACT.Copy, scale=MLA_SCALE)
                        last = fn(qabsS.rearrange("p b (h q) -> p b h q", h=H)[:, :, h, :],
                                  src[:, 256:T].rearrange("p (b q) -> p b q", b=NB), ACT.Copy, scale=MLA_SCALE)
                    elif key[0] == "g":
                        n = key[1]
                        if n:
                            store_gates()
                            act.wait_ge(gates_stored, 16 * n)
                        last = fn(estage, src[:, :], ACT.Exp, scale=-1.0)
                        gates["made"] += 1
                    elif key[0] == "sh":
                        m = key[1]
                        if m < 2:
                            last = fn(sh_sil[:, m, :], src[:, 0:T], ACT.Silu)
                        else:
                            last = fn(sh_up[:, m - 2, :], src[:, 0:T], ACT.Copy)
                    last.then_inc(free["P"], 1)
                    if key[0] == "g":
                        c = key[1] // TT
                        if key[1] % TT == TT - 1 and c + 2 < 6:
                            w_load(act, first_of["g"] + 2 * (c + 2))
                            w_load(act, first_of["g"] + 2 * (c + 2) + 1)
                elif ring == "V" and key[0] == "b":
                    n = (key[1] * 2 + key[2]) * TT + key[3]
                    if n == 0:
                        store_gates()
                        act.wait_ge(gates_stored, 16 * 6 * TT)
                        act.wait_ge(free["V"], done_at("V", "o", len(U) - 1))
                        for m in range(2):
                            act.dma_start(egate[m], gates_dram[m]).then_inc(gates_loaded[m], 16)
                    if n + 2 < 6 * TT:
                        act.wait_ge(free["V"], done_at(*st))
                        act.dma_start(egate[n % 2], gates_dram[n + 2]).then_inc(gates_loaded[n % 2], 16)
                elif ring == "rms":
                    act.wait_ge(sq_ready, 1)
                    link(fn(rst[:, 0:3], ssq[:, 0:3], ACT.Ln, bias=eps, scale=1.0 / QL))
                    link(fn(rst[:, 3:6], ssq[:, 3:6], ACT.Ln, bias=eps, scale=1.0 / KVL))
                    fn(rst[:, :], rst[:, :], ACT.Exp, scale=-0.5).then_inc(rstd_ready, 1)
                    act.wait_ge(nz_ready, 1)
                    link(fn(lft[:, 2, :], lft[:, 1, :], ACT.Exp))
                    fn(lft[:, 3, :], lft[:, 2, :], ACT.Ln, bias=one).then_inc(lse_ready, 1)
                elif ring == "S":
                    n = key[0]
                    rows, nk = unit_stage(n)
                    act.wait_ge(max_ready, n + 1)
                    if n >= 3:
                        act.wait_ge(done["T"], done_at("T", "p", n - 3))
                    fn(prob[n % 3][0:rows, 0:nk * P], ps["S"][n % 2][0:rows, 0:nk * P], ACT.Exp, bias=mx[0:rows, n:n + 1],
                       accum_out=sm[0:rows, n:n + 1]).then_inc(exp_ready, 1)
                    store_gates()
                elif ring == "ln1":
                    for j in range(TT):
                        act.wait_ge(lnv_ready, j + 1)
                        link(fn(rst[:, j:j + 1], rt[:, 0, 2 * j + 1:2 * j + 2], ACT.Ln, bias=eps))
                        fn(rst[:, j:j + 1], rst[:, j:j + 1], ACT.Exp, scale=-0.5).then_inc(rstd1_ready, 1)
                elif st == ("V", "shd", TT - 1, 1):
                    act.wait_ge(free["V"], done_at(*st))
                    act.dma_start(sum_rows, x_sb).then_inc(sum_begun, 16)
                elif st == ("V", "router", 2):
                    act.wait_ge(z_ready, 1)
                    fn(sel, sc, ACT.Exp, scale=-1.0).then_inc(ez_ready, 1)

            def expert(r, i, q):
                e, par = i * 4 + q, q % 2
                act.wait_ge(gate_done, E * r + e + 1)
                fn(sil[par], ps["P"][0][:, 0:2 * CAP].rearrange("p (m c) -> p m c", m=2), ACT.Silu).then_inc(silu_ready, 1)
                act.wait_ge(row_buffer_free, E * r + e + 1)
                act.wait_ge(info_ready, (E + AHEAD) * r + e + 1)
                for half in range(2):
                    act.wait_ge(down_done, 2 * (E * r + e) + half + 1)
                    fn(yo[par][0:CAP, half * 512:(half + 1) * 512], ps["V"][half][0:CAP, :], ACT.Copy, scale=info[0:CAP, q, 1:2])\
                        .then_inc(down_free, 1)

            def expert_round(r):
                with act.Fori(0, E // 4) as i:
                    for q in range(4):
                        expert(r, i, q)
            act.sem_inc(down_free, 2)
            rounds(act, expert_round)
            for j in range(TT):
                act.wait_ge(lnv_ready, TT + j + 1)
                link(fn(rst[:, j:j + 1], rt[:, 0, 2 * j + 1:2 * j + 2], ACT.Ln, bias=eps))
                fn(rst[:, j:j + 1], rst[:, j:j + 1], ACT.Exp, scale=-0.5).then_inc(rstd1_ready, 1)

        @block.vector
        def _(dve):
            V = nc.vector
            steps = {dve_step: 0, overflow_step: 0}
            now = [dve_step]

            def link(ins):
                steps[now[0]] += 1
                ins.then_inc(now[0], 1)
                dve.wait_ge(now[0], steps[now[0]])

            dve.wait_ge(cst_loaded, 16)

            def rope(out, src, cos, sin, t):
                a1, a2 = src[..., 0:16], src[..., 16:32]
                link(V.tensor_tensor(t[0], a1, cos, ALU.mult))
                link(V.tensor_tensor(t[1], a2, sin, ALU.mult))
                link(V.tensor_tensor(out[..., 0:16], t[0], t[1], ALU.subtract))
                link(V.tensor_tensor(t[0], a1, sin, ALU.mult))
                link(V.tensor_tensor(t[1], a2, cos, ALU.mult))
                link(V.tensor_tensor(out[..., 16:32], t[0], t[1], ALU.add))

            def prep(n):
                kind, g, i, q, rows, keys = U[n]
                if n == 0:
                    link(V.memset(qbd_fox, 0.0))
                    link(V.memset(qbd_mem, 0.0))
                if n >= 3:
                    dve.wait_ge(done["S"], n - 2)
                if kind == "fox" and (g == "s" or q == 0):
                    dve.wait_ge(free["V"], done_at("V", "c", i if g == "s" else "p"))
                if kind == "fox" and g == "p" and q == 0:
                    link(V.tensor_scalar(LH[i % 2], FX, cc("oh")[:, i:i + 1], None, ALU.mult))
                if g == "s" and kind == "mla":
                    if i == 0:
                        dve.wait_ge(logf_loaded, 16)
                        link(V.memset(LFc[0], 0.0))
                        link(V.memset(LFc[1], 0.0))
                    link(V.tensor_scalar(LFc[i % 2][:, :, 0:8], lfc_raw[:, 2 * i:2 * i + 2, :], -1.0, None, ALU.mult))
                    link(V.tensor_copy(LFc[i % 2][:, :, 32:40], lfc_raw[:, 2 * i:2 * i + 2, :]))
                if g == "s" and kind == "fox":
                    ts = slice(256 + NQ * i, 256 + NQ * (i + 1))
                    fx = FX[:, 0:NQ].unsqueeze(1).to_broadcast([P, H, NQ])
                    oh = cc("oh").unsqueeze(2).to_broadcast([P, H, NQ])
                    link(V.tensor_tensor(LH[0][:, 0:P].rearrange("p (h q) -> p h q", h=H), fx, oh, ALU.mult))
                    v = qbd_fox.rearrange("p (m c) -> p m c", c=160)
                    for half in range(2):
                        r = slice(half * 64, half * 64 + 64)
                        link(V.tensor_copy(v[r, :, half * NQ:(half + 1) * NQ], fqT[r, :, ts]))
                if g == "s" and kind == "mem":
                    ts = slice(256 + NQ * i, 256 + NQ * (i + 1))
                    v = qbd_mem.rearrange("p (m c) -> p m c", c=80)
                    link(V.tensor_copy(v[:, :, 0:NQ], mqT[:, :, ts]))
                dve.sem_inc(prep_ready, 1)

            def layer_norm(base, ready):
                for j in range(TT):
                    st6 = rt[:, 1, 16 * j:16 * j + 12]
                    link(V.bn_stats(st6[:, 0:6], x_sb[:, j, 0:512]))
                    link(V.bn_stats(st6[:, 6:12], x_sb[:, j, 512:D]))
                    V.bn_aggr(rt[:, 0, 2 * j:2 * j + 2], st6).then_inc(lnv_ready, 1)
                for j in range(TT):
                    dve.wait_ge(rstd1_ready, base + j + 1)
                    xv = x_sb[:, j, :]
                    link(V.tensor_scalar(xv, xv, rt[:, 0, 2 * j:2 * j + 1], rst[:, j:j + 1], ALU.subtract, ALU.mult))
                    link(V.tensor_tensor(xv, xv, lngb[:, 0:D], ALU.mult))
                    V.tensor_tensor(xv, xv, lngb[:, D:2 * D], ALU.add).then_inc(ready, 1)

            def route():
                link(V.memset(TGP, 0.0))
                dve.wait_ge(ez_ready, 1)
                link(V.tensor_scalar(sel, sel, 1.0, None, ALU.add))
                link(V.reciprocal(sc, sel))
                link(V.tensor_tensor(sel, sc, rb_b.unsqueeze(1).to_broadcast([P, TT, E]), ALU.add))
                for j in range(TT):
                    for g in range(NG):
                        ins = V.max(g8[:, j * NG + g, :], sel[:, j, g * 8:(g + 1) * 8])
                link(ins)
                link(V.tensor_tensor(gs, g8[:, :, 0], g8[:, :, 1], ALU.add))
                gk = [gs[:, j * 8:(j + 1) * 8].unsqueeze(1).to_broadcast([P, 8, 8]) for j in range(TT)]
                gi = [gs[:, j * 8:(j + 1) * 8].unsqueeze(2).to_broadcast([P, 8, 8]) for j in range(TT)]
                more = [masked[:, j, :].rearrange("p (i k) -> p i k", i=8) for j in range(TT)]
                same = [rep[:, j, :].rearrange("p (i k) -> p i k", i=8) for j in range(TT)]
                for j in range(TT):
                    V.tensor_tensor(more[j], gk[j], gi[j], ALU.is_gt)
                    ins = V.tensor_tensor(same[j], gk[j], gi[j], ALU.is_equal)
                link(ins)
                link(V.tensor_tensor(rep, rep, cc("before").unsqueeze(1).to_broadcast([P, TT, E]), ALU.mult))
                link(V.tensor_tensor(masked, masked, rep, ALU.add))
                for j in range(TT):
                    ins = V.tensor_reduce(gm[:, j * 8:(j + 1) * 8], more[j], AX, ALU.add)
                link(ins)
                link(V.tensor_scalar(gm, gm, float(TG), None, ALU.is_lt))
                keep = [gm[:, j * 8:(j + 1) * 8].unsqueeze(2).to_broadcast([P, 8, 8]) for j in range(TT)]
                grouped = [masked[:, j, :].rearrange("p (g c) -> p g c", g=8) for j in range(TT)]
                for j in range(TT):
                    ins = V.tensor_tensor(grouped[j], sel[:, j, :].rearrange("p (g c) -> p g c", g=8), keep[j], ALU.mult)
                link(ins)
                link(V.tensor_scalar(gm, gm, 1.0, 1e30, ALU.subtract, ALU.mult))
                for j in range(TT):
                    ins = V.tensor_tensor(grouped[j], grouped[j], keep[j], ALU.add)
                link(ins)
                for j in range(TT):
                    ins = V.max(t8[:, j, :], masked[:, j, :])
                link(ins)
                for j in range(TT):
                    ins = V.match_replace(rep[:, j, :], t8[:, j, :], masked[:, j, :], -3e38)
                link(ins)
                V.tensor_tensor(mask, rep, masked, ALU.not_equal).then_inc(mask_ready, 1)
                dve.wait_ge(mask_ready, 1)
                link(V.tensor_tensor(rep, sc, mask, ALU.mult))
                link(V.tensor_reduce(wsum, rep, AX, ALU.add))
                link(V.reciprocal(wsum, wsum))
                for j in range(TT):
                    V.tensor_scalar(tgp[:, j, 0:E, 1], rep[:, j, :], wsum[:, j:j + 1], 2.5, ALU.mult, ALU.mult)
                    ins = V.tensor_scalar(tgp[:, j, 0:E, 0], mask[:, j, :], 0.0, cc("tok")[:, j:j + 1], ALU.mult, ALU.add)
                link(ins)
                link(V.tensor_scalar(tgp[:, :, 0:E, 0], tgp[:, :, 0:E, 0], 1.0, None, ALU.add))

            def tables():
                dve.wait_ge(free["V"], done_at("V", "pos", TT - 1))
                link(V.scalar_tensor_tensor(rep, tmp3, 1.0, mask, ALU.add, ALU.mult))
                V.tensor_reduce(cmax, rep, mybir.AxisListType.XY, ALU.max).then_inc(count_ready, 1)
                link(V.memset(tgp[:, :, :, 2], -1.0))
                link(V.tensor_scalar(tgp[:, :, 0:E, 2], rep, -1.0, None, ALU.add))

            for st in PLAN:
                ring, key = st[0], st[1:]
                if ring == "T":
                    dve.wait_ge(done["T"], done_at(*st))
                    src = ps["T"][pos_in[st] % 2]
                    src4 = src[:, :].rearrange("p (k t) -> p k t", k=4)
                    if key[0] in ("x", "mem", "y", "x1"):
                        dst = {"x": xT, "mem": memT, "y": yT, "x1": xT}[key[0]]
                        _, j, half = key
                        last = V.tensor_copy(dst[:, half * 4:half * 4 + 4, j * P:(j + 1) * P], src4)
                    elif key[0] == "uk":
                        last = V.tensor_copy(wukT[0:64, key[1] * 4:key[1] * 4 + 4, :], src4[0:64])
                    elif key[0] == "lat":
                        ts = slice(key[1] * P, (key[1] + 1) * P)
                        V.tensor_copy(qnT[:, :, ts], src4[:, 0:2, :])
                        V.tensor_copy(latT[:, ts], src4[:, 2, :])
                        last = V.tensor_copy(krT[0:RD, ts], src4[0:RD, 3, :])
                    elif key[0] == "qr":
                        _, j, half = key
                        if j < 2:
                            last = V.tensor_copy(qrP[0:RD, half * 4:half * 4 + 4, j * P:(j + 1) * P], src4[0:RD])
                        else:
                            last = V.tensor_copy(
                                qrS[0:RD].rearrange("p b (h q) -> p h b q", h=H)[:, half * 4:half * 4 + 4],
                                src[0:RD, :].rearrange("p (h b q) -> p h b q", h=4, b=NB))
                    elif key[0] == "fk":
                        last = V.tensor_copy(fkT[:, :, key[1] * P:(key[1] + 1) * P], src4)
                    elif key[0] == "mk":
                        last = V.tensor_copy(mkT[:, :, key[1] * P:(key[1] + 1) * P], src4)
                    elif key[0] == "clat":
                        b = key[1]
                        n = next(i for i, u in enumerate(U) if u[:3] == ("mla", "s", b))
                        dve.wait_ge(done["S"], n - 2)
                        V.tensor_copy(latTc.rearrange("p (t c) -> p t c", t=2), src4[:, 0:2, :])
                        last = V.tensor_copy(krTc[0:RD].rearrange("p (t c) -> p t c", t=2), src4[0:RD, 2:4, :])
                    elif key[0] in ("cfk", "cmk"):
                        _, b, t = key
                        kd = "fox" if key[0] == "cfk" else "mem"
                        n = next(i for i, u in enumerate(U) if u[:3] == (kd, "s", b))
                        dve.wait_ge(done["S"], n - 2)
                        dst = fkTc if key[0] == "cfk" else mkTc
                        last = V.tensor_copy(dst[:, :, t * P:(t + 1) * P], src4)
                    elif key[0] == "p":
                        n = key[1]
                        rows, nk = unit_stage(n)
                        if n >= 2:
                            dve.wait_ge(done["V"], done_at("V", "o", n - 2))
                        if rows == P:
                            last = V.tensor_copy(pT[n % 2][:, 0:nk * P], src[:, 0:nk * P])
                        else:
                            last = V.tensor_copy(pT[n % 2].rearrange("p (t r) -> p t r", t=3)[:, 0:nk, 0:rows],
                                                 src4[:, 0:nk, 0:rows])
                    last.then_inc(free["T"], 1)
                elif ring == "P" and key[0] == "g":
                    dve.wait_ge(free["P"], done_at(*st))
                    e = estage
                    link(V.tensor_scalar(e, e, 1.0, None, ALU.add))
                    V.reciprocal(e, e).then_inc(gate_ready, 1)
                elif ring == "rms":
                    dve.wait_ge(free["P"], done_at("P", "lat", 2))
                    dve.wait_ge(vec_loaded, 48)
                    for j in range(TT):
                        link(V.tensor_tensor_reduce(scr, lat_raw[:, j, 0:QL], lat_raw[:, j, 0:QL], 1.0, 0.0,
                                                    ALU.mult, ALU.add, ssq[:, j:j + 1]))
                        ins = V.tensor_tensor_reduce(scr[:, 0:KVL], lat_raw[:, j, QL:QL + KVL], lat_raw[:, j, QL:QL + KVL],
                                                     1.0, 0.0, ALU.mult, ALU.add, ssq[:, 3 + j:4 + j])
                        if j < TT - 1:
                            link(ins)
                    ins.then_inc(sq_ready, 1)
                    z = lft[:, 0, :].rearrange("p (j h) -> p j h", j=TT)
                    link(V.tensor_tensor(z, lat_raw[:, :, 416:424], b_f_b.unsqueeze(1).to_broadcast([P, TT, 8]), ALU.add))
                    link(V.tensor_scalar(lft[:, 1, :], lft[:, 0, :], -1.0, None, ALU.mult))
                    V.tensor_tensor(lft[:, 1, :], lft[:, 0, :], lft[:, 1, :], ALU.min).then_inc(nz_ready, 1)
                    cosk, sink = rope_t[:, :, 0:16], rope_t[:, :, 16:32]
                    tmp = [rt[:, i, 0:48].rearrange("p (j c) -> p j c", j=TT) for i in range(2)]
                    rope(kr_rot, lat_raw[:, :, 384:416], cosk, sink, tmp)
                    dve.wait_ge(rstd_ready, 1)
                    for j in range(TT):
                        V.scalar_tensor_tensor(qn[:, j, :], lat_raw[:, j, 0:QL], rst[:, j:j + 1], gq_b, ALU.mult, ALU.mult)
                        ins = V.scalar_tensor_tensor(latn[:, j, :], lat_raw[:, j, QL:QL + KVL], rst[:, 3 + j:4 + j], gkv_b,
                                                     ALU.mult, ALU.mult)
                    ins.then_inc(lat_ready, 1)
                    link(V.memset(LFn, 0.0))
                    dve.wait_ge(lse_ready, 1)
                    link(V.tensor_scalar(lft[:, 0, :], lft[:, 0, :], 0.0, None, ALU.min))
                    lf_flat = lf_new.rearrange("p j h -> p (j h)")
                    link(V.tensor_tensor(lf_flat, lft[:, 0, :], lft[:, 3, :], ALU.subtract))
                    V.tensor_scalar(LFn[:, :, 0:8], lf_new, -1.0, None, ALU.mult)
                    V.tensor_copy(LFn[:, :, 32:40], lf_new).then_inc(logf_ready, 1)
                elif ring == "qrope":
                    j = key[0]
                    dve.wait_ge(free["P"], done_at("P", "qr", j))
                    c = rope_t[:, j, 0:16].unsqueeze(1).to_broadcast([P, H, 16])
                    s = rope_t[:, j, 16:32].unsqueeze(1).to_broadcast([P, H, 16])
                    tmp = [rt[:, i, 0:128].rearrange("p (h c) -> p h c", h=H) for i in range(2)]
                    rope(qr_rot[:, j, :].rearrange("p (h c) -> p h c", h=H), qr_tok[:, j, :].rearrange("p (h c) -> p h c", h=H),
                         c, s, tmp)
                    dve.sem_inc(qrope_ready, 1)
                elif ring == "prep":
                    prep(key[0])
                elif ring == "S":
                    n = key[0]
                    rows, nk = unit_stage(n)
                    dve.wait_ge(done["S"], n + 1)
                    V.tensor_reduce(mx[0:rows, n:n + 1], ps["S"][n % 2][0:rows, 0:nk * P], AX, ALU.max, negate=True)\
                        .then_inc(max_ready, 1)
                elif ring == "norm":
                    n = key[0]
                    rows, nk = unit_stage(n)
                    dve.wait_ge(exp_ready, n + 1)
                    dve.sem_inc(free["S"], 1)
                    link(V.reciprocal(rs[0:rows, n:n + 1], sm[0:rows, n:n + 1]))
                    pv = prob[n % 3][0:rows, 0:nk * P]
                    V.tensor_scalar(pv, pv, rs[0:rows, n:n + 1], None, ALU.mult).then_inc(norm_ready, 1)
                elif ring == "V":
                    dve.wait_ge(done["V"], done_at(*st))
                    src = ps["V"][pos_in[st] % 2]
                    if key[0] == "c":
                        w = 256 if key[1] == "p" else T
                        if key[1] == "p":
                            link(V.memset(FX, 1.0))
                            link(V.memset(FR, 0.0))
                            V.memset(FR[32:40, :], 1.0)
                            V.tensor_copy(FX[32:40, :], src[32:40, 0:256])
                        else:
                            n = next(i for i, u in enumerate(U) if u[:3] == ("fox", "s", key[1]))
                            dve.wait_ge(done["S"], n - 2)
                            q0 = 256 + NQ * key[1]
                            V.tensor_copy(FX[32:40, 0:NQ], src[32:40, q0:q0 + NQ])
                        last = V.tensor_copy(FR[0:32, 0:w], src[0:32, 0:w])
                    elif key[0] == "o":
                        kind, g, i, q, rows, keys = U[key[1]]
                        if kind == "mla":
                            if key[1] >= 2 and U[key[1] - 2][0] == "mla":
                                dve.wait_ge(done["V"], done_at("V", "ov", key[1] - 2))
                            elif g == "s" and i > 0:
                                dve.wait_ge(done["V"], done_at("V", "ov", key[1] - 3))
                            last = V.tensor_copy(olat[key[1] % 2], src[:, 0:P])
                        elif g == "p":
                            br = 1 if kind == "fox" else 2
                            h0, hn, blkk = ((i % 2) * 64, 64, i // 2) if kind == "fox" else (0, P, i)
                            last = V.tensor_copy(oT[h0:h0 + hn, br, blkk, q * P:(q + 1) * P], src[h0:h0 + hn, 0:P])
                        elif kind == "fox":
                            sv = src[:, 0:P].rearrange("p (m c) -> p m c", m=4)
                            ts = slice(256 + NQ * i, 256 + NQ * (i + 1))
                            V.tensor_copy(oT[0:64, 1, :, ts], sv[0:64, :, 0:NQ])
                            last = V.tensor_copy(oT[64:P, 1, :, ts], sv[64:P, :, NQ:2 * NQ])
                        else:
                            ts = slice(256 + NQ * i, 256 + NQ * (i + 1))
                            last = V.tensor_copy(oT[:, 2, :, ts], src[:, 0:64].rearrange("p (m c) -> p m c", m=4))
                    elif key[0] == "ov":
                        kind, g, i, q, rows, keys = U[key[1]]
                        if g == "p":
                            h0 = (i % 2) * 64
                            last = V.tensor_copy(oT[h0:h0 + 64, 0, i // 2, q * P:(q + 1) * P], src[h0:h0 + 64, 0:P])
                        else:
                            ts = slice(256 + NQ * i, 256 + NQ * (i + 1))
                            last = V.tensor_copy(oT[:, 0, :, ts], src[:, 0:64].rearrange("p (m c) -> p m c", m=4))
                    elif key[0] == "b":
                        _, br, cb, j = key
                        n = (br * 2 + cb) * TT + j
                        dve.wait_ge(gates_loaded[n % 2], 16 * (n // 2 + 1))
                        e = egate[n % 2]
                        yv = y[:, j, cb * 512:(cb + 1) * 512]
                        if br:
                            dve.wait_ge(free["V"], done_at("V", "b", br - 1, cb, j))
                        if br == 0:
                            last = V.tensor_tensor(yv, src[:, :], e, ALU.mult)
                        else:
                            link(V.tensor_tensor(e, src[:, :], e, ALU.mult))
                            last = V.tensor_tensor(yv, yv, e, ALU.add)
                    elif key[0] == "out":
                        _, j, half = key
                        cs = slice(half * 512, (half + 1) * 512)
                        last = V.scalar_tensor_tensor(x_sb[:, j, cs], x_sb[:, j, cs], ALPHA, src[:, :], ALU.mult, ALU.add)
                    elif key[0] == "router":
                        last = V.tensor_copy(sc[:, key[1], :], src[:, 0:E])
                    elif key[0] == "pos":
                        last = V.tensor_copy(tmp3[:, key[1], :], src[:, 0:E])
                    elif key[0] == "flag":
                        link(V.tensor_reduce(wsum[0:1, 0:1], src[0:1, 0:P], AX, ALU.max))
                        V.tensor_copy(flag_i[0:1, 0:1], wsum[0:1, 0:1]).then_inc(flag_ready, 1)
                        last = V.tensor_copy(wsum[0:1, 1:2], wsum[0:1, 0:1])
                    elif key[0] == "shd":
                        _, j, half = key
                        dve.wait_ge(x1_stored, 16)
                        cs = slice(half * 512, (half + 1) * 512)
                        last = V.scalar_tensor_tensor(x_sb[:, j, cs], x_sb[:, j, cs], ALPHA, src[:, :], ALU.mult, ALU.add)
                    last.then_inc(free["V"], 1)
                    if key == ("router", 2):
                        dve.wait_ge(free["V"], done_at(*st))
                        dve.sem_inc(z_ready, 1)
                elif ring == "ln1":
                    dve.wait_ge(free["V"], done_at("V", "out", 2, 1))
                    dve.wait_ge(ln_loaded, 32)
                    layer_norm(0, x1_ready)
                elif ring == "route":
                    route()
                elif ring == "tables":
                    tables()
                elif ring == "shact":
                    dve.wait_ge(free["P"], done_at("P", "sh", 3))
                    V.tensor_tensor(sh_sil, sh_sil, sh_up, ALU.mult).then_inc(hidden_ready, 1)

            def build_onehot(r, e, par):
                V.tensor_copy(pcol[par], tgp[:, :, bass.ds(e, 1), :].rearrange("p j o c -> p j (o c)")).then_inc(column_copied, 1)
                dve.wait_ge(column_copied, (E + AHEAD + 1) * r + e + 1)
                for j in range(TT):
                    ins = V.tensor_scalar(onehot[par][:, j, :], cc("iota"), pcol[par][:, j, 2:3], None, ALU.is_equal)
                ins.then_inc(onehot_built, 1)

            def copy_slots(r, e, par, q):
                n = (E + AHEAD) * r + e + 1
                dve.wait_ge(slots_done, n)
                out = ps["S"][par][0:CAP]
                V.tensor_scalar(empty[0:CAP], out[:, 0:1], 0.0, cc("unused", CAP), ALU.is_equal, ALU.mult).then_inc(empty_found, 1)
                V.tensor_copy(info[0:CAP, q, 1:2], out[:, 1:2])
                dve.wait_ge(empty_found, n)
                V.scalar_tensor_tensor(info[0:CAP, q, 0:1], out[:, 0:1], -1.0, empty[0:CAP], ALU.add, ALU.add).then_inc(info_ready, 1)
                dve.wait_ge(info_ready, n)
                V.tensor_copy(idx[0:CAP, q:q + 1], info[0:CAP, q, 0:1]).then_inc(idx_ready, 1)

            def take_turned(r, e, par):
                dve.wait_ge(xg_turned, 2 * ((E + 1) * r + e) + 1)
                V.tensor_copy(xgT[par][:, 0:4, :], ps["T"][0][:, 0:4 * CAP].rearrange("p (k c) -> p k c", k=4)).then_inc(xgT_ready, 1)
                dve.wait_ge(xg_turned, 2 * ((E + 1) * r + e) + 2)
                V.tensor_copy(xgT[par][:, 4:8, :], ps["T"][1][:, 0:4 * CAP].rearrange("p (k c) -> p k c", k=4)).then_inc(xgT_ready, 1)

            def expert(r, i, q):
                e, par = i * 4 + q, q % 2
                dve.wait_ge(silu_ready, E * r + e + 1)
                dve.wait_ge(gate_up_done, E * r + e + 1)
                V.tensor_tensor(hid[par], sil[par], ps["P"][1][:, 0:2 * CAP].rearrange("p (m c) -> p m c", m=2), ALU.mult)\
                    .then_inc(hid_ready, 1)
                take_turned(r, e + 1, 1 - par)
                V.tensor_copy(idx[0:CAP, 4 + q:5 + q], info[0:CAP, q, 0:1]).then_inc(dst_ready, 1)
                dve.wait_ge(down_free, 2 * (E * r + e + 1))
                copy_slots(r, e + AHEAD, 1 - par, (q + AHEAD) % 4)
                build_onehot(r, e + AHEAD + 1, par)

            def expert_round(r):
                if r:
                    now[0] = overflow_step
                    link(V.tensor_scalar(tgp[:, :, :, 2], tgp[:, :, :, 2], -float(CAP), None, ALU.add))
                build_onehot(r, 0, 0)
                build_onehot(r, 1, 1)
                if r:
                    dve.wait_ge(down_free, 2 * (E * r + 1))
                    for q in range(4):
                        dve.wait_ge(xg_loaded[q], 16 * GATHERS[q] * r)
                for e in range(AHEAD):
                    copy_slots(r, e, e % 2, e)
                    if e + 2 <= AHEAD:
                        build_onehot(r, e + 2, e % 2)
                take_turned(r, 0, 0)
                with dve.Fori(0, E // 4) as i:
                    for q in range(4):
                        expert(r, i, q)
                now[0] = dve_step
            rounds(dve, expert_round)
            dve.wait_ge(sum_loaded, 16)
            dve.wait_ge(ln2_loaded, 32)
            layer_norm(TT, out_ready)


_INS = ["x_prompt", "x_sample", "mem_prompt", "cache_mla_latent", "cache_mla_krope", "cache_fox_k", "cache_fox_v",
        "cache_fox_logf", "cache_mem_k", "cache_mem_v", "ln1_g", "ln1_b", "w_in", "b_f", "q_norm_g", "w_q_up",
        "kv_norm_g", "w_kv_up", "w_mem_k", "w_mem_v", "w_br_mla", "w_br_fox", "w_br_mem", "w_out", "ln2_g", "ln2_b",
        "w_router", "router_bias", "w_e_gate", "w_e_up", "w_e_down", "w_s_gate", "w_s_up", "w_s_down"]
_OUTS = [("y_prompt", (1, 256, 1024)), ("y_sample", (8, 16, 1024)), ("p_mla_latent", (1, 1, 256, 128)),
         ("p_mla_krope", (1, 1, 256, 32)), ("p_fox_k", (1, 1, 256, 8, 64)), ("p_fox_v", (1, 1, 256, 8, 64)),
         ("p_fox_logf", (1, 1, 256, 8)), ("p_mem_k", (1, 1, 256, 4, 128)), ("p_mem_v", (1, 1, 256, 4, 128)),
         ("s_mla_latent", (1, 8, 16, 128)), ("s_mla_krope", (1, 8, 16, 32)), ("s_fox_k", (1, 8, 16, 8, 64)),
         ("s_fox_v", (1, 8, 16, 8, 64)), ("s_fox_logf", (1, 8, 16, 8))]


def kernel(**inputs):
    import concourse.bacc as bacc
    from concourse.bass_utils import run_bass_kernel_spmd

    nc = bacc.Bacc("TRN2", target_bir_lowering=False, num_devices=1)
    arrays, a = {}, {}
    for name in _INS:
        v = np.ascontiguousarray(inputs[name])
        arrays[name] = v
        a[name] = nc.dram_tensor(name, v.shape, F32, kind="ExternalInput").ap()
    arrays["consts"] = constants()
    a["consts"] = nc.dram_tensor("consts", (P, NCST), F32, kind="ExternalInput").ap()
    outs = {n: nc.dram_tensor(n, s, F32, kind="ExternalOutput").ap() for n, s in _OUTS}
    build(nc, a, outs)
    r = run_bass_kernel_spmd(nc, [arrays], core_ids=[0])
    return tuple(r.results[0][n] for n, _ in _OUTS)
```
